# Optimizing a Trainium2 kernel written in Bass

```python
import math
import jax
import jax.numpy as jnp
from jax import lax
import numpy as np

D_MODEL = 1024
BATCH = 1
SEQ = 256
DEPTH = 4

CHUNK = 64
N_MIXERS = 3
N_LAYERS_A = (DEPTH + 2) // 3
N_LAYERS_B = (DEPTH + 1) // 3
N_LAYERS_C = DEPTH // 3
RMS_EPS = 1e-6
N_MOD = 6
D_FF = -(-8 * D_MODEL // (3 * 256)) * 256

M_D_INNER = 2 * D_MODEL
M_HEAD_DIM = 64
M_HEADS = M_D_INNER // M_HEAD_DIM
M_GROUPS = 8
M_D_STATE = 128
M_D_CONV = 4
M_CONV_DIM = M_D_INNER + 2 * M_GROUPS * M_D_STATE
M_D_IN_PROJ = M_D_INNER + M_CONV_DIM + M_HEADS

R_HEAD_DIM = 64
R_HEADS = D_MODEL // R_HEAD_DIM
R_DECAY_LORA = max(32, int(round(1.8 * D_MODEL ** 0.5 / 32)) * 32)
R_AAA_LORA = max(32, int(round(1.8 * D_MODEL ** 0.5 / 32)) * 32)
R_GATE_LORA = max(32, int(round(0.6 * D_MODEL ** 0.8 / 32)) * 32)
R_GN_EPS = 64e-5

F_HEAD_DIM = 64
F_HEADS = D_MODEL // F_HEAD_DIM
Q_BLOCK = 128

kernel_name = 'hybrid_ssd_rwkv7_fox_adaln_trunk'

def rms_norm(x, w, eps=RMS_EPS):
    xf = x.astype(jnp.float32)
    y = xf * lax.rsqrt(jnp.mean(xf * xf, axis=-1, keepdims=True) + eps)
    return (y * w.astype(jnp.float32)).astype(x.dtype)

def causal_depthwise_conv(u, w, b):
    k = w.shape[0]
    out = lax.conv_general_dilated(
        u, w[:, None, :], window_strides=(1,), padding=[(k - 1, 0)],
        dimension_numbers=('NWC', 'WIO', 'NWC'), feature_group_count=u.shape[-1])
    return out + b

def segsum(a):
    t = a.shape[-1]
    a_rep = jnp.broadcast_to(a[..., None], a.shape + (t,))
    a_rep = jnp.where(jnp.tril(jnp.ones((t, t), bool), -1), a_rep, 0.0)
    ss = jnp.cumsum(a_rep, axis=-2)
    return jnp.where(jnp.tril(jnp.ones((t, t), bool)), ss, -jnp.inf)

def ssd_chunked(x, dt, A, Bm, Cm):
    b, s, h, p = x.shape
    g, n = Bm.shape[-2:]
    j = h // g
    nc = s // CHUNK
    xd = (x.astype(jnp.float32) * dt[..., None]).reshape(b, nc, CHUNK, g, j, p)
    a = (dt * A).reshape(b, nc, CHUNK, g, j).transpose(0, 3, 4, 1, 2)
    Bc = Bm.astype(jnp.float32).reshape(b, nc, CHUNK, g, n)
    Cc = Cm.astype(jnp.float32).reshape(b, nc, CHUNK, g, n)
    a_cs = jnp.cumsum(a, axis=-1)
    Lmat = jnp.exp(segsum(a))
    scores = jnp.einsum('bclgn,bcmgn->bgclm', Cc, Bc)
    y_diag = jnp.einsum('bgclm,bgjclm,bcmgjp->bclgjp', scores, Lmat, xd)
    decay_states = jnp.exp(a_cs[..., -1:] - a_cs)
    states = jnp.einsum('bclgn,bgjcl,bclgjp->bcgjpn', Bc, decay_states, xd)
    chunk_decay = jnp.exp(a_cs[..., -1])

    def step(carry, inp):
        st, dec = inp
        return carry * dec[..., None, None] + st, carry

    init = jnp.zeros((b, g, j, p, n), jnp.float32)
    _, prev = lax.scan(step, init, (jnp.moveaxis(states, 1, 0), jnp.moveaxis(chunk_decay, -1, 0)))
    prev = jnp.moveaxis(prev, 0, 1)
    y_off = jnp.einsum('bclgn,bcgjpn,bgjcl->bclgjp', Cc, prev, jnp.exp(a_cs))
    return (y_diag + y_off).reshape(b, s, h, p).astype(x.dtype)

def mamba2_mixer(h, in_w, conv_w, conv_b, dt_bias, A_log, d_skip, norm_w, out_w):
    b, s, _ = h.shape
    zxbcdt = h @ in_w
    z, xbc, dt = jnp.split(zxbcdt, [M_D_INNER, M_D_INNER + M_CONV_DIM], axis=-1)
    xbc = jax.nn.silu(causal_depthwise_conv(xbc, conv_w, conv_b))
    xs, Bm, Cm = jnp.split(xbc, [M_D_INNER, M_D_INNER + M_GROUPS * M_D_STATE], axis=-1)
    xs = xs.reshape(b, s, M_HEADS, M_HEAD_DIM)
    Bm = Bm.reshape(b, s, M_GROUPS, M_D_STATE)
    Cm = Cm.reshape(b, s, M_GROUPS, M_D_STATE)
    dt = jax.nn.softplus((dt + dt_bias).astype(jnp.float32))
    A = -jnp.exp(A_log.astype(jnp.float32))
    y = ssd_chunked(xs, dt, A, Bm, Cm) + xs * d_skip[:, None]
    yg = (y.reshape(b, s, M_D_INNER) * jax.nn.silu(z)).reshape(b, s, M_GROUPS, -1)
    yg = rms_norm(yg, norm_w.reshape(M_GROUPS, -1)).reshape(b, s, M_D_INNER)
    return yg @ out_w

def rwkv7_mixer(h, mix, w_rkv, w0, w1, w2, a0, a1, a2, g1, g2, k_k, k_a, r_k, lnx_w, lnx_b, out_w):
    b, s, d = h.shape
    f32 = jnp.float32
    dx = jnp.pad(h, ((0, 0), (1, 0), (0, 0)))[:, :-1] - h
    xs = h[None] + dx[None] * mix[:, None, None, :]
    r, k, v = jnp.einsum('nbsd,nde->nbse', xs[:3], w_rkv)
    w_log = -jax.nn.softplus(-(w0 + jnp.tanh(xs[3] @ w1) @ w2)) - 0.5
    decay = jnp.exp(-jnp.exp(w_log.astype(f32)))
    a = jax.nn.sigmoid(a0 + (xs[4] @ a1) @ a2)
    g = jax.nn.sigmoid(xs[5] @ g1) @ g2

    def heads(t):
        return t.reshape(b, s, R_HEADS, R_HEAD_DIM).astype(f32)

    kk = heads(k * k_k)
    kk = kk / jnp.maximum(jnp.linalg.norm(kk, axis=-1, keepdims=True), 1e-12)
    k = k * (1 + (a - 1) * k_a)
    rh, kh, vh, ah, wh = heads(r), heads(k), heads(v), heads(a), heads(decay)

    def step(state, inp):
        r_t, w_t, k_t, v_t, kk_t, bb_t = inp
        sa = jnp.einsum('bhij,bhj->bhi', state, -kk_t)
        state = (state * w_t[:, :, None, :] + sa[..., None] * bb_t[:, :, None, :]
                 + v_t[..., None] * k_t[:, :, None, :])
        return state, jnp.einsum('bhij,bhj->bhi', state, r_t)

    tm = lambda t: jnp.moveaxis(t, 1, 0)
    s0 = jnp.zeros((b, R_HEADS, R_HEAD_DIM, R_HEAD_DIM), f32)
    _, y = lax.scan(step, s0, (tm(rh), tm(wh), tm(kh), tm(vh), tm(kk), tm(kk * ah)))
    y = jnp.moveaxis(y, 0, 1)
    mu = jnp.mean(y, axis=-1, keepdims=True)
    var = jnp.mean(jnp.square(y - mu), axis=-1, keepdims=True)
    y = ((y - mu) * lax.rsqrt(var + R_GN_EPS)).reshape(b, s, d) * lnx_w + lnx_b
    bonus = jnp.sum(rh * kh * r_k, axis=-1, keepdims=True) * vh
    y = (y + bonus.reshape(b, s, d)).astype(h.dtype)
    return (y * g) @ out_w

def fox_mixer(h, qkvf_w, fgate_b, q_norm_w, k_norm_w, out_w):
    b, s, d = h.shape
    proj = h @ qkvf_w
    q, k, v, f = jnp.split(proj, [d, 2 * d, 3 * d], axis=-1)
    q = rms_norm(q.reshape(b, s, F_HEADS, F_HEAD_DIM), q_norm_w).transpose(0, 2, 1, 3)
    k = rms_norm(k.reshape(b, s, F_HEADS, F_HEAD_DIM), k_norm_w).transpose(0, 2, 1, 3)
    v = v.reshape(b, s, F_HEADS, F_HEAD_DIM).transpose(0, 2, 1, 3)
    log_f = jax.nn.log_sigmoid((f + fgate_b).astype(jnp.float32))
    cum = jnp.cumsum(log_f, axis=1).transpose(0, 2, 1)
    scale = F_HEAD_DIM ** -0.5
    outs = []
    for qb in range(s // Q_BLOCK):
        q0 = qb * Q_BLOCK
        kend = q0 + Q_BLOCK
        logits = jnp.einsum('bhqd,bhkd->bhqk', q[:, :, q0:kend], k[:, :, :kend]).astype(jnp.float32) * scale
        logits = logits + cum[:, :, q0:kend, None] - cum[:, :, None, :kend]
        mask = (q0 + jnp.arange(Q_BLOCK))[:, None] >= jnp.arange(kend)[None, :]
        p = jax.nn.softmax(jnp.where(mask, logits, -jnp.inf), axis=-1)
        outs.append(jnp.einsum('bhqk,bhkd->bhqd', p.astype(v.dtype), v[:, :, :kend]))
    o = jnp.concatenate(outs, axis=2).transpose(0, 2, 1, 3).reshape(b, s, d)
    return o @ out_w

def swiglu_ffn(h, w1, w3, w2):
    return (jax.nn.silu(h @ w1) * (h @ w3)) @ w2

def setup_inputs(seed: int = 0) -> dict:
    key = jax.random.key(seed)
    keys = jax.random.split(key, 48)
    counter = [0]
    f32 = jnp.float32

    def nk():
        counter[0] += 1
        return keys[counter[0] - 1]

    def nrm(shape, scale):
        return jax.random.normal(nk(), shape, f32) * scale

    def unif(shape, lo, hi):
        return jax.random.uniform(nk(), shape, f32, lo, hi)

    D = D_MODEL
    na, nb, nc = N_LAYERS_A, N_LAYERS_B, N_LAYERS_C
    inv = lambda n: n ** -0.5
    x = nrm((BATCH, SEQ, D), 1.0)
    c = nrm((BATCH, D), 1.0)
    ada_w = nrm((DEPTH, D, N_MOD * D), 0.1 * inv(D))
    ada_b = nrm((DEPTH, N_MOD * D), 0.02)
    norm1_w = 1.0 + nrm((DEPTH, D), 0.02)
    norm2_w = 1.0 + nrm((DEPTH, D), 0.02)
    ffn_w1 = nrm((DEPTH, D, D_FF), inv(D))
    ffn_w3 = nrm((DEPTH, D, D_FF), inv(D))
    ffn_w2 = nrm((DEPTH, D_FF, D), inv(D_FF))
    m_in_w = nrm((na, D, M_D_IN_PROJ), inv(D))
    m_conv_w = nrm((na, M_D_CONV, M_CONV_DIM), inv(M_D_CONV))
    m_conv_b = nrm((na, M_CONV_DIM), 0.02)
    dt0 = jnp.exp(unif((na, M_HEADS), math.log(1e-3), math.log(1e-1)))
    m_dt_bias = dt0 + jnp.log(-jnp.expm1(-dt0))
    m_A_log = jnp.log(unif((na, M_HEADS), 1.0, 16.0))
    m_D = 1.0 + nrm((na, M_HEADS), 0.1)
    m_norm_w = 1.0 + nrm((na, M_D_INNER), 0.02)
    m_out_w = nrm((na, M_D_INNER, D), inv(M_D_INNER))
    r_mix = unif((nb, 6, D), 0.0, 1.0)
    r_w_rkv = nrm((nb, 3, D, D), inv(D))
    r_w0 = unif((nb, D), -6.0, 1.0)
    r_w1 = nrm((nb, D, R_DECAY_LORA), inv(D))
    r_w2 = nrm((nb, R_DECAY_LORA, D), 0.5 * inv(R_DECAY_LORA))
    r_a0 = nrm((nb, D), 0.1)
    r_a1 = nrm((nb, D, R_AAA_LORA), inv(D))
    r_a2 = nrm((nb, R_AAA_LORA, D), 0.5 * inv(R_AAA_LORA))
    r_g1 = nrm((nb, D, R_GATE_LORA), inv(D))
    r_g2 = nrm((nb, R_GATE_LORA, D), inv(R_GATE_LORA))
    r_k_k = 0.85 + nrm((nb, D), 0.02)
    r_k_a = 1.0 + nrm((nb, D), 0.02)
    r_r_k = nrm((nb, R_HEADS, R_HEAD_DIM), 0.1)
    r_lnx_w = 1.0 + nrm((nb, D), 0.02)
    r_lnx_b = nrm((nb, D), 0.02)
    r_out_w = nrm((nb, D, D), inv(D))
    f_qkvf_w = nrm((nc, D, 3 * D + F_HEADS), inv(D))
    f_fgate_b = unif((nc, F_HEADS), 1.0, 5.0)
    f_q_norm_w = 1.0 + nrm((nc, F_HEAD_DIM), 0.02)
    f_k_norm_w = 1.0 + nrm((nc, F_HEAD_DIM), 0.02)
    f_out_w = nrm((nc, D, D), inv(D))
    return {
        'x': x, 'c': c, 'ada_w': ada_w, 'ada_b': ada_b,
        'norm1_w': norm1_w, 'norm2_w': norm2_w,
        'ffn_w1': ffn_w1, 'ffn_w3': ffn_w3, 'ffn_w2': ffn_w2,
        'm_in_w': m_in_w, 'm_conv_w': m_conv_w, 'm_conv_b': m_conv_b,
        'm_dt_bias': m_dt_bias, 'm_A_log': m_A_log, 'm_D': m_D,
        'm_norm_w': m_norm_w, 'm_out_w': m_out_w,
        'r_mix': r_mix, 'r_w_rkv': r_w_rkv, 'r_w0': r_w0, 'r_w1': r_w1, 'r_w2': r_w2,
        'r_a0': r_a0, 'r_a1': r_a1, 'r_a2': r_a2, 'r_g1': r_g1, 'r_g2': r_g2,
        'r_k_k': r_k_k, 'r_k_a': r_k_a, 'r_r_k': r_r_k,
        'r_lnx_w': r_lnx_w, 'r_lnx_b': r_lnx_b, 'r_out_w': r_out_w,
        'f_qkvf_w': f_qkvf_w, 'f_fgate_b': f_fgate_b,
        'f_q_norm_w': f_q_norm_w, 'f_k_norm_w': f_k_norm_w, 'f_out_w': f_out_w,
    }

def reference(x, c, ada_w, ada_b, norm1_w, norm2_w, ffn_w1, ffn_w3, ffn_w2,
              m_in_w, m_conv_w, m_conv_b, m_dt_bias, m_A_log, m_D, m_norm_w, m_out_w,
              r_mix, r_w_rkv, r_w0, r_w1, r_w2, r_a0, r_a1, r_a2, r_g1, r_g2,
              r_k_k, r_k_a, r_r_k, r_lnx_w, r_lnx_b, r_out_w,
              f_qkvf_w, f_fgate_b, f_q_norm_w, f_k_norm_w, f_out_w):
    cond = jax.nn.silu(c)
    ia = ib = ic = 0
    for i in range(DEPTH):
        mod = (cond @ ada_w[i] + ada_b[i])[:, None, :]
        sh1, sc1, gt1, sh2, sc2, gt2 = jnp.split(mod, N_MOD, axis=-1)
        h = rms_norm(x, norm1_w[i]) * (1 + sc1) + sh1
        kind = i % N_MIXERS
        if kind == 0:
            y = mamba2_mixer(h, m_in_w[ia], m_conv_w[ia], m_conv_b[ia], m_dt_bias[ia],
                             m_A_log[ia], m_D[ia], m_norm_w[ia], m_out_w[ia])
            ia += 1
        elif kind == 1:
            y = rwkv7_mixer(h, r_mix[ib], r_w_rkv[ib], r_w0[ib], r_w1[ib], r_w2[ib],
                            r_a0[ib], r_a1[ib], r_a2[ib], r_g1[ib], r_g2[ib],
                            r_k_k[ib], r_k_a[ib], r_r_k[ib], r_lnx_w[ib], r_lnx_b[ib], r_out_w[ib])
            ib += 1
        else:
            y = fox_mixer(h, f_qkvf_w[ic], f_fgate_b[ic], f_q_norm_w[ic], f_k_norm_w[ic], f_out_w[ic])
            ic += 1
        x = x + (1 + gt1) * y
        h = rms_norm(x, norm2_w[i]) * (1 + sc2) + sh2
        x = x + (1 + gt2) * swiglu_ffn(h, ffn_w1[i], ffn_w3[i], ffn_w2[i])
    return x


_drawn_inputs = setup_inputs


def setup_inputs(seed=0):
    import zlib

    import numpy as np

    out = dict(_drawn_inputs(seed))
    spreads = {}
    factors = {'r_w1': 4.009,
     'r_w2': 4.121,
     'r_a0': 2.889,
     'r_k_k': 8.0,
     'r_k_a': 4.964,
     'r_lnx_w': 6.085,
     'r_lnx_b': 5.798,
     'f_q_norm_w': 8.0,
     'f_k_norm_w': 8.0}
    for name, (base, spread) in spreads.items():
        noise = np.random.default_rng([zlib.crc32(name.encode()), seed]).standard_normal(out[name].shape)
        drawn = base * np.exp(spread * noise) if base else spread * noise
        out[name] = jnp.asarray(drawn.astype(out[name].dtype))
    for name, factor in factors.items():
        out[name] = (out[name] * factor).astype(out[name].dtype)
    return out
```

```python
from contextlib import ExitStack
import math

import numpy as np
import concourse.bass as bass
from concourse import mybir

ALU = mybir.AluOpType
ACT = mybir.ActivationFunctionType
AX = mybir.AxisListType
F32 = mybir.dt.float32

P = 128
D = 1024
S = 256
DEPTH = 4
KD = D // P
TT = S // P
NB = 512
DFF = 2816
KF = DFF // P
M_IN = 2048
M_KT = M_IN // P
M_XBC = 4096
M_G = 8
M_H = 32
HD = 64
R_H = 16
LORA = 64
LORA_G = 160
CH = 64
NC = S // CH
EPS = 1e-6
R_GN_EPS = 64e-5
E_HALF = math.exp(-0.5)
SLOT = 4096
RING = 4
NADA = 12
NEG = -1e30

VECTORS = [("c", KD), ("norm1_w", 4 * KD), ("norm2_w", 4 * KD), ("m_conv_w", 256), ("m_conv_b", 64),
           ("m_norm_w", 32), ("r_mix", 48), ("r_w0", 8), ("r_a0", 8), ("r_k_k", 8), ("r_k_a", 8),
           ("r_r_k", 8), ("r_lnx_w", 8), ("r_lnx_b", 8)]
COL = {}
_at = 0
for _n, _r in VECTORS:
    COL[_n] = _at
    _at += _r
NVEC = _at
NVT = -(-NVEC // P)


N_ROWS = 9
VEC_LAYOUT = {"c": "a d -> (a d)", "norm1_w": "a d -> (a d)", "norm2_w": "a d -> (a d)", "m_conv_w": "a b d -> (a b d)",
              "m_conv_b": "a d -> (a d)", "m_norm_w": "a d -> (a d)", "r_mix": "a b d -> (a b d)", "r_r_k": "a b d -> (a b d)"}
for _n in ("r_w0", "r_a0", "r_k_k", "r_k_a", "r_lnx_w", "r_lnx_b"):
    VEC_LAYOUT[_n] = "a d -> (a d)"


def vector_parts():
    out = []
    for name, n in VECTORS:
        r = 0
        while r < n:
            at = COL[name] + r
            m = min(n - r, P - at % P)
            out.append((name, r, m, at % P, at // P))
            r += m
    return out


def trunk(nc, t, out):
    with ExitStack() as ctx:
        def sb(name, shape):
            return ctx.enter_context(nc.sbuf_tensor(name, shape, F32))

        def sem(name):
            return ctx.enter_context(nc.semaphore(name))

        x = sb("x", [P, TT, D])
        hT = sb("hT", [P, KD, S])
        ring = sb("ring", [P, RING, SLOT])
        gate = sb("gate", [P, 2, D])
        vcol = sb("vcol", [P, NVEC])
        mcol = sb("mcol", [P, 32])
        nsc = sb("nsc", [P, 2, KD])
        ident = sb("ident", [P, P])
        ones = sb("ones", [P, P])
        halves = sb("halves", [P, P])
        upto = sb("upto", [P, 384])
        after = sb("after", [P, P])
        neg = sb("neg", [P, 384])
        level = sb("level", [P, 6, P])
        before_c = sb("before_c", [P, P])
        upto_c = sb("upto_c", [P, P])
        wnar = sb("wnar", [P, KD, M_H])
        small = sb("small", [P, 8])
        epsc = sb("epsc", [P, 3])
        dskip = sb("dskip", [P, 2, M_KT])
        qkw = sb("qkw", [P, 2])
        rowb = sb("rowb", [P, 160])
        pend = sb("pend", [P, KD, NC])
        ARENA = 25600
        arena = sb("arena", [P, ARENA])
        psum_acc = [ctx.enter_context(nc.psum_tensor(f"psum_acc{i}", [P, NB], F32)) for i in range(4)]
        psum_act = [ctx.enter_context(nc.psum_tensor(f"psum_act{i}", [P, NB], F32)) for i in range(2)]
        psum_dve = [ctx.enter_context(nc.psum_tensor(f"psum_dve{i}", [P, NB], F32)) for i in range(2)]

        def carve(off, *dims):
            n = int(np.prod(dims))
            assert off + n <= ARENA, (off, n)
            v = arena[:, off:off + n]
            if len(dims) == 2:
                v = v.rearrange("p (a b) -> p a b", a=dims[0])
            elif len(dims) == 3:
                v = v.rearrange("p (a b c) -> p a b c", a=dims[0], b=dims[1])
            elif len(dims) == 4:
                v = v.rearrange("p (a b c d) -> p a b c d", a=dims[0], b=dims[1], c=dims[2])
            return v

        vrow = carve(8192, NVT, P)
        xn = carve(0, TT, D)
        gT = carve(2048, KF, S)
        ada = carve(ARENA - 6144, 6144)
        xbcT = carve(0, 32, S)
        xd = carve(8192, TT, M_IN)
        sqz = carve(8192, M_KT, S)
        scT = carve(12288, M_G, 384)
        dec = carve(15360, 3, 384)
        gm = carve(16512, 4, 384)
        segw = carve(18048, 2, 2, P)
        zs = carve(18560, 2, NB)
        rsm = carve(19584, 2, S)
        dtv = carve(20096, 5, TT, M_H)
        fqk = carve(0, 2, KD, S)
        fv = carve(4096, TT, D)
        foT = carve(6144, KD, S)
        fsq = carve(8192, 2, NB)
        frs = carve(9216, 2, NB)
        fsegw = carve(10240, 2, 384)
        flg = carve(11008, 4, 384)
        fpT = carve(12544, 4, 384)
        fst = carve(14080, 4, 2, R_H)
        ffv = carve(14208, 5, TT, R_H)
        A8 = [carve(2048 * i, KD, S) for i in range(8)]
        r_dx, r_xsA, r_xsB, r_s, r_a, r_r, r_k, r_v = A8
        r_XT = carve(16384, 32, HD)
        wk = [[carve(18432 + 2560 * q + 512 * i, 4, P) for i in range(5)] for q in range(2)]
        r_mk = [[carve(23552 + 1024 * q + 512 * i, 4, P) for i in range(2)] for q in range(2)]
        r_R = carve(23552, 2, KD, HD)
        r_SA = carve(24576, 2, KD, HD)
        r_hid = carve(18432, 3, S)
        r_vt = hT[:, :, :].rearrange("p a b -> p (a b)").rearrange("p (t d) -> p t d", t=TT)
        r_bt = arena[:, 0:2048].rearrange("p (t d) -> p t d", t=TT)
        r_kt = arena[:, 4096:6144].rearrange("p (t d) -> p t d", t=TT)
        r_U = arena[:, 2048:4096].rearrange("p (k t d) -> p k t d", k=KD, t=TT)
        r_Arb = arena[:, 8192:10240].rearrange("p (h t d) -> p h t d", h=R_H, t=TT)
        r_XT4 = arena[:, 16384:18432].rearrange("p (h t d) -> p h t d", h=R_H, t=TT)
        r_S = carve(18432, KD, HD)
        r_hgS = sb("r_hgS", [P, 2, S])

        act_full, act_free = sem("act_bank_full"), sem("act_bank_free")
        dve_full, dve_free = sem("dve_bank_full"), sem("dve_bank_free")
        acc_full, acc_free = sem("acc_full"), sem("acc_free")
        act_step, dve_step, pool_step = sem("act_step"), sem("dve_step"), sem("pool_step")
        landed = [sem(f"slot_landed{i}") for i in range(RING)]
        ada_used, down_slot = sem("ada_slot_used"), sem("down_slot_used")
        ada_zero, ada_bias = sem("ada_zeroed"), sem("ada_bias_landed")
        mixer_done = sem("mixer_done")
        consts, vec_landed, x_landed, row_landed = sem("consts"), sem("vectors_landed"), sem("x_landed"), sem("rows_landed")
        cond_ready, mod_ready = sem("cond_ready"), sem("mod_ready")
        x_ready, rstd_ready, xn_ready = sem("x_ready"), sem("rstd_ready"), sem("xn_ready")
        wdt_landed = sem("narrow_weight_landed")
        dt_raw, dt_e, dt_done = sem("dt_raw"), sem("dt_e"), sem("dt_done")
        xbc_silu, seg_ready, decay_ready, gmat_ready = sem("xbc_silu"), sem("seg_ready"), sem("decay_ready"), sem("gmat_ready")
        z_ready, yz_ready, sq_ready, rs_ready, yn_ready = (sem("z_ready"), sem("yz_ready"), sem("sq_ready"),
                                                          sem("rs_ready"), sem("yn_ready"))
        f_sq, f_rs, f_qk = sem("fox_sq"), sem("fox_rs"), sem("fox_qk_ready")
        f_max, f_exp, f_norm = sem("fox_max"), sem("fox_exp"), sem("fox_norm")
        xs_ready = sem("rwkv_xs_ready")
        r_v2a, r_a2v = sem("rwkv_dve_to_act"), sem("rwkv_act_to_dve")
        r_v2p, r_a2p, ns_ready = sem("rwkv_dve_to_pe"), sem("rwkv_act_to_pe"), sem("rwkv_ns_ready")
        out_landed = sem("out_landed")
        block = ctx.enter_context(nc.Block())

        loads, key_of = [], {}

        def add(key, *parts):
            key_of[key] = len(loads)
            loads.append(parts)

        def slot(n):
            return ring[:, n % RING, :]

        def rows(w, n0, nn):
            return w[:, n0:n0 + nn].rearrange("(k p) n -> p k n", p=P)

        def load_ada(l, s):
            add(("ada", l, s), (slice(0, 4096), rows(t["ada_w"][l], s * 512, 512), P, 512))

        def load_ffn(l):
            for i in range(KF // 2):
                add(("up", l, i), (slice(0, 2048), rows(t["ffn_w1"][l], i * 256, 256), P, 256),
                    (slice(2048, 4096), rows(t["ffn_w3"][l], i * 256, 256), P, 256))
                if l + 1 < DEPTH:
                    load_ada(l + 1, i)
            for i in range(-(-KF // 4)):
                load_down(("down2", l), t["ffn_w2"][l], i, KF)
                if i == 0 and l + 1 < DEPTH:
                    load_ada(l + 1, 11)

        def load_down(key, w, i, nk):
            k = min(4, nk - 4 * i)
            add((*key, i), (slice(0, k * 1024), w[512 * i:512 * i + 128 * k, :].rearrange("(k p) n -> p k n", p=P), P, 1024))

        for s in range(NADA):
            load_ada(0, s)
        for l in range(DEPTH):
            if l % 3 == 0:
                o = l // 3
                for i in range(8):
                    add(("xbc", o, i), (slice(0, 4096), rows(t["m_in_w"][o], M_IN + i * 512, 512), P, 512))
                for i in range(4):
                    add(("z", o, i), (slice(0, 4096), rows(t["m_in_w"][o], i * 512, 512), P, 512))
                for i in range(4):
                    load_down(("mout", o), t["m_out_w"][o], i, M_KT)
            elif l % 3 == 1:
                add(("lora",), (slice(0, 512), rows(t["r_w1"][0], 0, LORA), P, LORA),
                    (slice(512, 1024), rows(t["r_a1"][0], 0, LORA), P, LORA),
                    (slice(1024, 2304), rows(t["r_g1"][0], 0, LORA_G), P, LORA_G),
                    (slice(2304, 3328), t["r_w2"][0], (0, 64), 0),
                    (slice(2304, 3328), t["r_a2"][0], (64, 128), 0))
                for j in range(3):
                    for i in range(2):
                        add(("rkv", j, i), (slice(0, 4096), rows(t["r_w_rkv"][0, j], i * 512, 512), P, 512))
                add(("g2",), (slice(0, 1024), t["r_g2"][0, 0:128], (0, 128), 0),
                    (slice(1024, 2048), t["r_g2"][0, 128:160], (0, 32), 0))
                for i in range(2):
                    load_down(("rout",), t["r_out_w"][0], i, KD)
            else:
                for i in range(6):
                    add(("qkv", i), (slice(0, 4096), rows(t["f_qkvf_w"][0], i * 512, 512), P, 512))
                for i in range(2):
                    load_down(("fout",), t["f_out_w"][0], i, KD)
            load_ffn(l)

        arrive_at, total = [], [0] * RING
        for n, parts in enumerate(loads):
            total[n % RING] += 16 * len(parts)
            arrive_at.append(total[n % RING])
        n_vec_dmas = len(vector_parts())
        release = {}
        mark = {}

        def arrive(eng, key):
            n = key_of[key]
            eng.wait_ge(landed[n % RING], arrive_at[n])
            return n

        @block.tensor
        def _(pe):
            jobs = {"act": 0, "dve": 0}

            def open_bank(who):
                n = jobs[who]
                if n >= 2:
                    pe.wait_ge(act_free if who == "act" else dve_free, n - 1)
                return (psum_act if who == "act" else psum_dve)[n % 2]

            def close_bank(who, last):
                jobs[who] += 1
                last.then_inc(act_full if who == "act" else dve_full, 1)
                return jobs[who]

            def note(name):
                mark[name] = (jobs["act"], jobs["dve"])

            def read_out(who, n):
                pe.wait_ge(act_free if who == "act" else dve_free, n)

            def all_read_out():
                if jobs["act"]:
                    pe.wait_ge(act_free, jobs["act"])
                if jobs["dve"]:
                    pe.wait_ge(dve_free, jobs["dve"])

            def mm(o, l, r, start=True, stop=True):
                return nc.tensor.matmul(o, l, r, start=start, stop=stop, skip_group_check=True)

            def tr(o, i, n=P):
                return nc.tensor.transpose(o, i, ident[0:n, 0:n])

            def freed(key, who):
                release[key_of[key]] = ({"act": act_full, "dve": dve_full}[who], jobs[who])

            down_count = [0]

            def down(key, nk, lhs, ready=None):
                d = down_count[0]
                down_count[0] += 1
                if d:
                    pe.wait_ge(acc_free, 4 * d)
                for k in range(nk):
                    if ready:
                        ready(k)
                    if k % 4 == 0:
                        n = arrive(pe, (*key, k // 4))
                    w = slot(n)[:, (k % 4) * D:(k % 4 + 1) * D]
                    for tt in range(TT):
                        for nh in range(2):
                            last = mm(psum_acc[tt * 2 + nh][:, :], lhs(k, tt), w[:, nh * NB:(nh + 1) * NB],
                                      start=(k == 0), stop=(k == nk - 1))
                            if k == nk - 1:
                                last.then_inc(acc_full, 1)
                    if k == nk - 1:
                        release[n] = (acc_full, 4 * d + 4)
                    elif k % 4 == 3:
                        last.then_inc(down_slot, 1)
                        down_slots[0] += 1
                        release[n] = (down_slot, down_slots[0])

            down_slots = [0]

            def feature_tiles(key, i, who, jobs_of=2, src=None):
                n = arrive(pe, key)
                w = slot(n).rearrange("p (k c) -> p k c", k=KD)
                for j in range(jobs_of):
                    b = open_bank(who)
                    for u in range(2):
                        for k in range(KD):
                            c = (2 * j + u) * P
                            last = mm(b[:, u * S:(u + 1) * S], w[:, k, c:c + P], src[:, k, :], k == 0, k == KD - 1)
                    close_bank(who, last)
                freed(key, who)

            def modulation(l):
                pe.wait_ge(ada_used, NADA * (l + 1))
                note(("mod", l))
                for m in (2, 5):
                    for nh in range(2):
                        b = open_bank("dve")
                        close_bank("dve", mm(b[:, :], ones[:, :], ada[:, m * D + nh * NB:m * D + (nh + 1) * NB]))
                b = open_bank("dve")
                for j, m in enumerate((0, 1, 3, 4)):
                    for k in range(KD):
                        last = mm(b[:, j * KD + k:j * KD + k + 1], ada[:, m * D + k * P:m * D + (k + 1) * P], ones[:, 0:1])
                close_bank("dve", last)

            norms = [0]

            def norm(l, which):
                note(("norm", l, which))
                for j in range(4):
                    who = ("act", "dve")[j % 2]
                    b = open_bank(who)
                    for u in range(2):
                        for tt in range(TT):
                            if j == 0 and u == 0:
                                pe.wait_ge(xn_ready, 2 * norms[0] + tt + 1)
                            last = tr(b[:, (2 * u + tt) * P:(2 * u + tt + 1) * P], xn[:, tt, (2 * j + u) * P:(2 * j + u + 1) * P])
                    close_bank(who, last)
                norms[0] += 1
                all_read_out()

            def ffn(l):
                note(("ffn", l))
                for i in range(KF // 2):
                    n = arrive(pe, ("up", l, i))
                    w = slot(n).rearrange("p (m k c) -> p m k c", m=2, k=KD)
                    for m, who in enumerate(("act", "dve")):
                        b = open_bank(who)
                        for u in range(2):
                            for k in range(KD):
                                last = mm(b[:, u * S:(u + 1) * S], w[:, m, k, u * P:(u + 1) * P], hT[:, k, :], k == 0, k == KD - 1)
                        close_bank(who, last)
                    freed(("up", l, i), "dve")
                j0 = mark[("ffn", l)][1]
                down(("down2", l), KF, lambda k, tt: gT[:, k, tt * P:(tt + 1) * P],
                     lambda k: read_out("dve", j0 + k // 2 + 1))

            def mamba(o):
                note(("mamba", o))
                pe.wait_ge(wdt_landed, 16 * (o + 1 if o == 0 else 3))
                b = open_bank("dve")
                for tt in range(TT):
                    for k in range(KD):
                        last = mm(b[:, tt * M_H:(tt + 1) * M_H], hT[:, k, tt * P:(tt + 1) * P], wnar[:, k, :], k == 0, k == KD - 1)
                close_bank("dve", last)
                note(("conv", o))
                for i in range(8):
                    feature_tiles(("xbc", o, i), i, "dve", src=hT)
                note(("xT", o))
                pe.wait_ge(xbc_silu, 16 * o + 8)
                for j in range(8):
                    b = open_bank("dve")
                    for tt in range(TT):
                        for u in range(2):
                            last = tr(b[:, (2 * tt + u) * P:(2 * tt + u + 1) * P], xbcT[:, 2 * j + u, tt * P:(tt + 1) * P])
                    close_bank("dve", last)
                note(("score", o))
                pe.wait_ge(xbc_silu, 16 * o + 16)
                for g in range(M_G):
                    b = open_bank("dve")
                    mm(b[:, 0:256], xbcT[:, 16 + g, 0:P], xbcT[:, 24 + g, :])
                    close_bank("dve", mm(b[:, 256:384], xbcT[:, 16 + g, P:S], xbcT[:, 24 + g, P:S]))
                note(("head", o))
                for h in range(M_H + 4):
                    if h < M_H:
                        pe.wait_ge(seg_ready, (M_H + R_H) * o + h + 1)
                        b = open_bank("act")
                        mm(b[:, 0:256], segw[:, h % 2, 0, :], upto[:, 0:256], True, False)
                        mm(b[:, 128:256], dtv[:, 4, 1, h:h + 1].broadcast_to([P, P]), upto[:, 0:P], False, True)
                        close_bank("act", mm(b[:, 256:384], segw[:, h % 2, 1, :], upto[:, 0:P]))
                    if h >= 4 and h % 2 == 0:
                        p = (h - 4) // 2
                        pe.wait_ge(gmat_ready, M_H * o + 2 * p + 2)
                        b = open_bank("dve")
                        for q in range(2):
                            hh, oo = 2 * p + q, slice(HD * q, HD * q + HD)
                            mm(b[oo, 0:256], xd[:, 0, hh * HD:(hh + 1) * HD], gm[:, hh % 4, 0:256], True, False)
                            last = mm(b[oo, 128:256], xd[:, 1, hh * HD:(hh + 1) * HD], gm[:, hh % 4, 256:384], False, True)
                        close_bank("dve", last)
                note(("z", o))
                for i in range(4):
                    feature_tiles(("z", o, i), i, "act", src=hT)
                note(("ssum", o))
                for g in range(M_G):
                    pe.wait_ge(sq_ready, M_G * o + g + 1)
                    b = open_bank("act")
                    mm(b[:, 0:256], ones[:, :], sqz[:, 2 * g, :], True, False)
                    close_bank("act", mm(b[:, 0:256], ones[:, :], sqz[:, 2 * g + 1, :], False, True))
                down(("mout", o), M_KT, lambda k, tt: xbcT[:, k, tt * P:(tt + 1) * P],
                     lambda k: pe.wait_ge(yn_ready, M_G * o + k // 2 + 1))

            def fox():
                note("fox")
                pe.wait_ge(wdt_landed, 32)
                b = open_bank("dve")
                for tt in range(TT):
                    for k in range(KD):
                        last = mm(b[:, tt * R_H:(tt + 1) * R_H], hT[:, k, tt * P:(tt + 1) * P], wnar[:, k, 0:R_H], k == 0, k == KD - 1)
                close_bank("dve", last)
                sq = 0

                def head_sums(j):
                    pe.wait_ge(f_sq, j + 1)
                    b = open_bank("act")
                    close_bank("act", mm(b[:, :], halves[:, :], fsq[:, j % 2, :]))
                for i in range(4):
                    n = arrive(pe, ("qkv", i))
                    w = slot(n).rearrange("p (k c) -> p k c", k=KD)
                    for j in range(2):
                        b = open_bank("act")
                        for u in range(2):
                            for k in range(KD):
                                last = mm(b[:, u * S:(u + 1) * S], w[:, k, (2 * j + u) * P:(2 * j + u + 1) * P], hT[:, k, :], k == 0, k == KD - 1)
                        close_bank("act", last)
                        if j == 1:
                            freed(("qkv", i), "act")
                        if sq:
                            head_sums(sq - 1)
                        sq += 1
                head_sums(7)
                for i in range(2):
                    n = arrive(pe, ("qkv", 4 + i))
                    w = slot(n).rearrange("p (k c) -> p k c", k=KD)
                    for tt in range(TT):
                        b = open_bank("dve")
                        for k in range(KD):
                            last = mm(b[:, :], hT[:, k, tt * P:(tt + 1) * P], w[:, k, :], k == 0, k == KD - 1)
                        close_bank("dve", last)
                    freed(("qkv", 4 + i), "dve")
                note("foxhead")
                pe.wait_ge(f_qk, 8)
                for h in range(R_H + 4):
                    if h < R_H:
                        t8, r0 = h // 2, HD * (h % 2)
                        rr = slice(r0, r0 + HD)
                        pe.wait_ge(seg_ready, M_H + h + 1)
                        b = open_bank("dve")
                        sw = fsegw[:, h % 2, :]
                        mm(b[:, 0:P], upto[:, 0:P], sw[:, 0:P], True, False)
                        mm(b[:, 0:P], fqk[rr, 0, t8, 0:P], fqk[rr, 1, t8, 0:P], False, True)
                        mm(b[:, P:384], upto[:, 0:P], sw[:, P:384], True, False)
                        mm(b[:, P:2 * P], ones[:, :], sw[:, 0:P], False, False)
                        close_bank("dve", mm(b[:, P:384], fqk[rr, 0, t8, P:S], fqk[rr, 1, t8, :], False, True))
                    if 2 <= h < R_H + 2:
                        hh = h - 2
                        pe.wait_ge(f_norm, hh + 1)
                        b = open_bank("act")
                        for c in range(3):
                            last = tr(b[:, c * P:(c + 1) * P], flg[:, hh % 4, c * P:(c + 1) * P])
                        close_bank("act", last)
                    if h >= 4 and h % 2 == 0:
                        p = (h - 4) // 2
                        read_out("act", mark["foxhead"][0] + 2 * p + 2)
                        b = open_bank("dve")
                        for q in range(2):
                            hh, oo = 2 * p + q, slice(HD * q, HD * q + HD)
                            mm(b[oo, 0:256], fv[:, 0, hh * HD:(hh + 1) * HD], fpT[:, hh % 4, 0:256], True, False)
                            last = mm(b[oo, P:256], fv[:, 1, hh * HD:(hh + 1) * HD], fpT[:, hh % 4, 256:384], False, True)
                        close_bank("dve", last)
                all_read_out()
                down(("fout",), KD, lambda k, tt: foT[:, k, tt * P:(tt + 1) * P])

            def rwkv():
                note("rwkv")
                n = arrive(pe, ("lora",))
                w1 = slot(n)[:, 0:512].rearrange("p (k c) -> p k c", k=KD)
                a1 = slot(n)[:, 512:1024].rearrange("p (k c) -> p k c", k=KD)
                g1 = slot(n)[:, 1024:2304].rearrange("p (k c) -> p k c", k=KD)
                w2 = slot(n)[:, 2304:3328]
                pe.wait_ge(xs_ready, 1)
                b = open_bank("act")
                for k in range(KD):
                    last = mm(b[0:64, 0:S], w1[:, k, :], r_xsA[:, k, :], k == 0, k == KD - 1)
                close_bank("act", last)
                pe.wait_ge(xs_ready, 2)
                b = open_bank("act")
                for k in range(KD):
                    last = mm(b[64:128, 0:S], a1[:, k, :], r_xsB[:, k, :], k == 0, k == KD - 1)
                close_bank("act", last)
                pe.wait_ge(xs_ready, 3)
                b = open_bank("act")
                for k in range(KD):
                    mm(b[:, 0:S], g1[:, k, 0:P], r_xsA[:, k, :], k == 0, k == KD - 1)
                for k in range(KD):
                    last = mm(b[0:32, S:2 * S], g1[:, k, P:LORA_G], r_xsA[:, k, :], k == 0, k == KD - 1)
                close_bank("act", last)
                read_out("act", mark["rwkv"][0] + 2)
                for m in range(2):
                    pr = slice(64 * m, 64 * m + 64)
                    for j in range(4):
                        b = open_bank("act")
                        for u in range(2):
                            c = (2 * j + u) * P
                            last = mm(b[:, u * S:(u + 1) * S], w2[pr, c:c + P], r_hid[pr, 0, :])
                        close_bank("act", last)
                freed(("lora",), "act")
                for j, xs in enumerate((r_xsB, r_xsA, r_xsB)):
                    pe.wait_ge(xs_ready, 4 + j)
                    note(("rkv", j))
                    for i in range(2):
                        feature_tiles(("rkv", j, i), i, "dve" if j == 1 else "act", src=xs)
                note("vt")
                read_out("act", mark["vt"][0])
                for j in range(4):
                    b = open_bank("act")
                    for tt in range(TT):
                        for u in range(2):
                            last = tr(b[:, (2 * tt + u) * P:(2 * tt + u + 1) * P], r_v[:, 2 * j + u, tt * P:(tt + 1) * P])
                    close_bank("act", last)
                note("knorm")
                for j in range(4):
                    pe.wait_ge(r_a2p, j + 1)
                    b = open_bank("act")
                    close_bank("act", mm(b[:, :], halves[:, :], arena[:, 4096 + NB * j:4096 + NB * (j + 1)]))
                note("bonus")
                pe.wait_ge(r_v2p, 1)
                for j in range(4):
                    b = open_bank("dve")
                    close_bank("dve", mm(b[:, :], halves[:, :], arena[:, 8192 + NB * j:8192 + NB * (j + 1)]))
                note("bkt")
                pe.wait_ge(r_v2p, 2)
                for src in (r_xsA, r_k):
                    for j in range(4):
                        b = open_bank("act")
                        for tt in range(TT):
                            for u in range(2):
                                last = tr(b[:, (2 * tt + u) * P:(2 * tt + u + 1) * P], src[:, 2 * j + u, tt * P:(tt + 1) * P])
                        close_bank("act", last)
                note("grams")
                KKd, Bi, Ki, Rd = r_s, r_xsA, r_k, r_r
                for B in range(4):
                    def gram(q, lh, rh):
                        pr = slice(64 * q, 64 * q + 64)
                        b = open_bank("dve")
                        for i in range(2):
                            for tt in range(TT):
                                ts = slice(tt * P, (tt + 1) * P)
                                last = mm(b[:, (2 * i + tt) * P:(2 * i + tt + 1) * P], lh[pr, 2 * B + i, ts], rh[pr, 2 * B + i, ts])
                        return close_bank("dve", last)
                    gr = {}
                    for q in range(2):
                        gr[q] = [gram(q, KKd, Bi), gram(q, Bi, Rd), gram(q, Ki, KKd), gram(q, Ki, Rd)]
                    for q in range(2):
                        read_out("dve", gr[q][2])
                        b = open_bank("act")
                        for i in range(2):
                            for tt in range(TT):
                                h = 2 * (2 * B + i) + q
                                last = mm(b[:, (2 * i + tt) * HD:(2 * i + tt + 1) * HD], r_mk[q][0][:, 2 * i + tt, :],
                                          r_vt[:, tt, h * HD:(h + 1) * HD])
                        close_bank("act", last)
                        read_out("dve", gr[q][3])
                        b = open_bank("act")
                        for i in range(2):
                            for tt in range(TT):
                                h = 2 * (2 * B + i) + q
                                last = mm(b[64 * q:64 * q + 64, (2 * i + tt) * P:(2 * i + tt + 1) * P],
                                          r_vt[:, tt, h * HD:(h + 1) * HD], r_mk[q][1][:, 2 * i + tt, :])
                        close_bank("act", last)
                    zr = {}
                    for q in range(2):
                        N_, Ns, X_, Z_, P_ = wk[q]
                        pe.wait_ge(ns_ready, 12 * B + q + 1)
                        b = open_bank("dve")
                        for c in range(4):
                            last = tr(b[:, c * P:(c + 1) * P], Ns[:, c, :])
                        zr[q] = close_bank("dve", last)
                    for lv in range(1, 6):
                        pj = {}
                        for q in range(2):
                            N_, Ns, X_, Z_, P_ = wk[q]
                            pe.wait_ge(ns_ready, 12 * B + 2 * lv + q + 1)
                            read_out("dve", zr[q])
                            b = open_bank("act")
                            for c in range(4):
                                last = mm(b[:, c * P:(c + 1) * P], Ns[:, c, :], Z_[:, c, :])
                            pj[q] = close_bank("act", last)
                        for q in range(2):
                            N_, Ns, X_, Z_, P_ = wk[q]
                            read_out("act", pj[q])
                            b = open_bank("dve")
                            for c in range(4):
                                last = mm(b[:, c * P:(c + 1) * P], X_[:, c, :], P_[:, c, :])
                            zr[q] = close_bank("dve", last)
                            if lv < 5:
                                b = open_bank("dve")
                                for c in range(4):
                                    last = mm(b[:, c * P:(c + 1) * P], P_[:, c, :], X_[:, c, :])
                                zr[q] = close_bank("dve", last)
                note("chunks")
                all_read_out()
                for c in range(NC):
                    tt, par = c // 2, c % 2
                    pr = slice(64 * par, 64 * par + 64)
                    cs = slice(c * CH, (c + 1) * CH)
                    if c:
                        read_out("dve", jobs["dve"])
                    for q in range(2):
                        qr = slice(64 * q, 64 * q + 64)
                        b = open_bank("dve")
                        for k in range(KD):
                            last = mm(b[pr, k * HD:(k + 1) * HD], KKd[qr, k, cs], r_S[qr, k, :])
                        close_bank("dve", last)
                    rj = jobs["dve"]
                    for q in range(2):
                        qr = slice(64 * q, 64 * q + 64)
                        b = open_bank("dve")
                        for k in range(KD):
                            last = mm(b[qr, k * HD:(k + 1) * HD], r_S[qr, k, :], Rd[qr, k, cs])
                        close_bank("dve", last)
                    read_out("dve", rj)
                    for q in range(2):
                        b = open_bank("act")
                        for k in range(KD):
                            last = mm(b[pr, k * HD:(k + 1) * HD], r_XT4[pr, 2 * k + q, tt, :], r_R[pr, q, k, :])
                        close_bank("act", last)
                    read_out("act", jobs["act"])
                    b = open_bank("dve")
                    for k in range(KD):
                        for q in range(2):
                            last = mm(b[64 * q:64 * q + 64, k * HD:(k + 1) * HD], r_SA[pr, q, k, :], r_Arb[pr, 2 * k + q, tt, :])
                    close_bank("dve", last)
                    if c < NC - 1:
                        b = open_bank("dve")
                        for k in range(KD):
                            for q in range(2):
                                h, o2 = 2 * k + q, b[64 * q:64 * q + 64, k * HD:(k + 1) * HD]
                                mm(o2, r_bt[pr, tt, h * HD:(h + 1) * HD], r_SA[pr, q, k, :], True, False)
                                last = mm(o2, r_kt[pr, tt, h * HD:(h + 1) * HD], r_vt[pr, tt, h * HD:(h + 1) * HD], False, True)
                        close_bank("dve", last)
                note("gn")
                all_read_out()
                for j in range(4):
                    b = open_bank("dve")
                    close_bank("dve", mm(b[:, :], halves[:, :], arena[:, 12288 + NB * j:12288 + NB * (j + 1)]))
                for j in range(4):
                    pe.wait_ge(r_a2p, 4 + j + 1)
                    b = open_bank("act")
                    close_bank("act", mm(b[:, :], halves[:, :], arena[:, NB * j:NB * (j + 1)]))
                n = arrive(pe, ("g2",))
                for j in range(4):
                    b = open_bank("dve")
                    for u in range(2):
                        cc = slice((2 * j + u) * P, (2 * j + u + 1) * P)
                        mm(b[:, u * S:(u + 1) * S], slot(n)[:, 0:1024][:, cc], r_hgS[:, 0, :], True, False)
                        last = mm(b[:, u * S:(u + 1) * S], slot(n)[0:32, 1024:2048][:, cc], r_hgS[0:32, 1, :], False, True)
                    close_bank("dve", last)
                freed(("g2",), "dve")
                j0 = jobs["dve"]
                down(("rout",), KD, lambda k, tt: r_k[:, k, tt * P:(tt + 1) * P], lambda k: read_out("dve", j0 - 3 + k // 2))

            pe.wait_ge(consts, 1)
            pe.wait_ge(vec_landed, 16 * n_vec_dmas)
            for v in range(NVT):
                r = min(P, NVEC - v * P)
                b = open_bank("act")
                close_bank("act", tr(b[:, 0:r], vrow[0:r, v, :], r))
            modulation(0)
            for l in range(DEPTH):
                norm(l, 0)
                if l % 3 == 0:
                    mamba(l // 3)
                elif l % 3 == 1:
                    rwkv()
                else:
                    fox()
                norm(l, 1)
                ffn(l)
                if l + 1 < DEPTH:
                    modulation(l + 1)

        @block.vector
        def _(dve):
            V = nc.vector
            counts = {}
            job = [0]

            def tell(ins, s=dve_step):
                counts[s.name] = counts.get(s.name, 0) + 1
                ins.then_inc(s, 1)
                dve.wait_ge(s, counts[s.name])

            def take():
                dve.wait_ge(dve_full, job[0] + 1)
                return psum_dve[job[0] % 2]

            def give(ins):
                job[0] += 1
                ins.then_inc(dve_free, 1)
                dve.wait_ge(dve_free, job[0])

            def flat(v):
                return v.rearrange("p a b -> p (a b)")

            def col(name, i, n=1):
                return vcol[:, COL[name] + i:COL[name] + i + n]

            def wide(name, i, n=KD):
                return col(name, i, n).unsqueeze(2).broadcast_to([P, n, S])

            def adaln(l, s):
                n = arrive(dve, ("ada", l, s))
                w = slot(n).rearrange("p (k c) -> p k c", k=KD)
                for k in range(KD):
                    for hf in range(2):
                        o = ada[:, s * 512 + hf * 256:s * 512 + hf * 256 + 256]
                        ins = V.scalar_tensor_tensor(out=o, in0=w[:, k, hf * 256:hf * 256 + 256], scalar=col("c", k),
                                                     in1=o, op0=ALU.mult, op1=ALU.add)
                        if k == KD - 1 and hf == 1:
                            tell(ins, ada_used)
                        else:
                            counts["dve_step"] = counts.get("dve_step", 0) + 1
                            ins.then_inc(dve_step, 1)
                            if counts["dve_step"] > 1:
                                dve.wait_ge(dve_step, counts["dve_step"] - (1 if k < KD - 1 or hf == 0 else 0))
                release[n] = (ada_used, NADA * l + s + 1)

            def modulation(l):
                for g in range(2):
                    for nh in range(2):
                        b = take()
                        give(V.tensor_scalar(gate[:, g, nh * NB:(nh + 1) * NB], b[:, :], 1.0, None, ALU.add))
                b = take()
                give(V.tensor_copy(mcol[:, :], b[:, 0:32]))
                for w in range(2):
                    ins = V.scalar_tensor_tensor(out=nsc[:, w, :], in0=mcol[:, 16 * w + 8:16 * w + 16], scalar=1.0,
                                                 in1=col(f"norm{w + 1}_w", l * KD, KD), op0=ALU.add, op1=ALU.mult)
                    tell(ins, mod_ready if w else dve_step)

            norms = [0]

            def norm(l, which):
                norms[0] += 1
                dve.wait_ge(rstd_ready, norms[0])
                for tt in range(TT):
                    tell(V.tensor_scalar(xn[:, tt, :], x[:, tt, :], small[:, 4 + tt:5 + tt], None, ALU.mult), xn_ready)
                for j in (1, 3):
                    b = take()
                    for u in range(2):
                        k = 2 * j + u
                        ins = V.tensor_scalar(hT[:, k, :], b[:, u * S:(u + 1) * S], nsc[:, which, k:k + 1],
                                              mcol[:, 16 * which + k:16 * which + k + 1], ALU.mult, ALU.add)
                        give(ins) if u else tell(ins)

            res = [0]

            def residual(g):
                for tt in range(TT):
                    for nh in range(2):
                        b = psum_acc[2 * tt + nh]
                        dve.wait_ge(acc_full, 4 * res[0] + 2 * tt + nh + 1)
                        tell(V.tensor_tensor(b[:, :], b[:, :], gate[:, g, nh * NB:(nh + 1) * NB], ALU.mult))
                        xs = x[:, tt, nh * NB:(nh + 1) * NB]
                        tell(V.tensor_tensor(xs, xs, b[:, :], ALU.add), acc_free)
                res[0] += 1

            def ffn(l):
                for i in range(KF // 2):
                    b = take()
                    dve.wait_ge(act_free, mark[("ffn", l)][0] + i + 1)
                    v = flat(gT[:, 2 * i:2 * i + 2, :])
                    give(V.tensor_tensor(v, v, b[:, :], ALU.mult))
                    if l + 1 < DEPTH:
                        if i == 0:
                            dve.wait_ge(ada_bias, 16 * (l + 2))
                        adaln(l + 1, i)
                if l + 1 < DEPTH:
                    adaln(l + 1, 11)
                residual(1)

            def mamba(o):
                m0 = mark[("mamba", o)]
                b = take()
                give(V.tensor_tensor(dtv[:, 0], b[:, 0:TT * M_H].rearrange("p (t h) -> p t h", t=TT),
                                     rowb[:, o * 32:o * 32 + 32].unsqueeze(1).broadcast_to([P, TT, M_H]), ALU.add))
                for j in range(16):
                    b = take()
                    for tap in range(4):
                        sft = 3 - (3 - tap)
                        for u in range(2):
                            c = 2 * j + u
                            w = col("m_conv_w", o * 128 + (3 - tap) * 32 + c)
                            if tap == 0:
                                ins = V.tensor_scalar(xbcT[:, c, :], b[:, u * S:(u + 1) * S], w, col("m_conv_b", o * 32 + c),
                                                      ALU.mult, ALU.add)
                            else:
                                ins = V.scalar_tensor_tensor(out=xbcT[:, c, sft:S], in0=b[:, u * S:(u + 1) * S - sft], scalar=w,
                                                             in1=xbcT[:, c, sft:S], op0=ALU.mult, op1=ALU.add)
                            give(ins) if (tap == 3 and u == 1) else tell(ins)
                dve.wait_ge(dt_e, o + 1 if o == 0 else 3)
                tell(V.scalar_tensor_tensor(out=dtv[:, 3], in0=dtv[:, 0], scalar=0.0, in1=dtv[:, 2], op0=ALU.max, op1=ALU.add))
                tell(V.scalar_tensor_tensor(out=dtv[:, 4], in0=dtv[:, 3], scalar=-1.0,
                                            in1=rowb[:, 64 + o * 32:96 + o * 32].unsqueeze(1).broadcast_to([P, TT, M_H]),
                                            op0=ALU.mult, op1=ALU.mult))
                for j in range(8):
                    b = take()
                    for tt in range(TT):
                        ins = V.tensor_tensor(xd[:, tt, 256 * j:256 * j + 256].rearrange("p (h d) -> p h d", h=4),
                                              b[:, tt * 256:(tt + 1) * 256].rearrange("p (h d) -> p h d", h=4),
                                              dtv[:, 3, tt, 4 * j:4 * j + 4].unsqueeze(2).broadcast_to([P, 4, HD]), ALU.mult)
                        give(ins) if tt else tell(ins)
                for g in range(M_G):
                    b = take()
                    give(V.tensor_tensor(scT[:, g, :], b[:, 0:384], upto[:, :], ALU.mult))
                a0 = mark[("head", o)][0]

                def seg(h):
                    for tt in range(TT):
                        tell(V.tensor_scalar(segw[:, h % 2, tt, :], after[:, :], dtv[:, 4, tt, h:h + 1], None, ALU.mult),
                             seg_ready if tt else dve_step)

                def pair_out(p):
                    b = take()
                    give(V.scalar_tensor_tensor(out=xbcT[:, p, :], in0=xbcT[:, p, :], scalar=dskip[:, o, p:p + 1],
                                                in1=b[:, 0:256], op0=ALU.mult, op1=ALU.add))
                seg(0)
                seg(1)
                for h in range(M_H):
                    if h >= 4 and h % 2 == 0:
                        pair_out((h - 4) // 2)
                    dve.wait_ge(act_free, a0 + h + 1)
                    tell(V.tensor_tensor(gm[:, h % 4, :], dec[:, h % 3, :], scT[:, h // 4, :], ALU.mult), gmat_ready)
                    if h + 2 < M_H:
                        seg(h + 2)
                pair_out(14)
                pair_out(15)
                for g in range(M_G):
                    dve.wait_ge(act_free, mark[("z", o)][0] + g + 1)
                    tell(V.tensor_tensor(flat(xbcT[:, 2 * g:2 * g + 2, :]), flat(xbcT[:, 2 * g:2 * g + 2, :]), zs[:, g % 2, :], ALU.mult), yz_ready)
                for g in range(M_G):
                    dve.wait_ge(rs_ready, M_G * o + g + 1)
                    for u in range(2):
                        c = 2 * g + u
                        tell(V.scalar_tensor_tensor(out=xbcT[:, c, :], in0=xbcT[:, c, :], scalar=col("m_norm_w", o * 16 + c),
                                                    in1=rsm[:, g % 2, :], op0=ALU.mult, op1=ALU.mult), yn_ready if u else dve_step)

            def fox():
                b = take()
                give(V.tensor_tensor(ffv[:, 0], b[:, 0:TT * R_H].rearrange("p (t h) -> p t h", t=TT),
                                     rowb[:, 128:144].unsqueeze(1).broadcast_to([P, TT, R_H]), ALU.add))
                dve.wait_ge(dt_e, 2)
                tell(V.scalar_tensor_tensor(out=ffv[:, 3], in0=ffv[:, 0], scalar=0.0, in1=ffv[:, 2], op0=ALU.min, op1=ALU.subtract))
                for i in range(8):
                    dve.wait_ge(f_rs, i + 1)
                    m, j = i // 4, i % 4
                    v = flat(fqk[:, m, 2 * j:2 * j + 2, :])
                    tell(V.scalar_tensor_tensor(out=v, in0=v, scalar=qkw[:, m:m + 1], in1=frs[:, i % 2, :], op0=ALU.mult, op1=ALU.mult), f_qk)
                for i in range(2):
                    for tt in range(TT):
                        b = take()
                        give(V.tensor_copy(fv[:, tt, i * NB:(i + 1) * NB], b[:, :]))
                a0 = mark["foxhead"][0]

                def seg(h):
                    tell(V.tensor_scalar(fsegw[:, h % 2, 0:P], after[:, :], ffv[:, 3, 0, h:h + 1], None, ALU.mult))
                    tell(V.tensor_scalar(fsegw[:, h % 2, P:2 * P], ones[:, :], ffv[:, 3, 1, h:h + 1], None, ALU.mult))
                    tell(V.tensor_scalar(fsegw[:, h % 2, 2 * P:], after[:, :], ffv[:, 3, 1, h:h + 1], None, ALU.mult), seg_ready)

                def normalise(h):
                    dve.wait_ge(f_exp, h + 1)
                    tell(V.reciprocal(fst[:, 3, :, h], fst[:, 2, :, h]))
                    for blk, r in enumerate((slice(0, P), slice(P, 384))):
                        tell(V.tensor_scalar(flg[:, h % 4, r], flg[:, h % 4, r], fst[:, 3, blk, h:h + 1], None, ALU.mult), f_norm if blk else dve_step)
                seg(0)
                seg(1)
                for h in range(R_H + 4):
                    if h < R_H:
                        b = take()
                        if h >= 4:
                            dve.wait_ge(act_full, a0 + h - 3)
                        for blk, r in enumerate((slice(0, P), slice(P, 384))):
                            ins = V.tensor_tensor_reduce(flg[:, h % 4, r], b[:, r], neg[:, r], 1.0, -3e38, ALU.add, ALU.max,
                                                         fst[:, 0, blk, h:h + 1])
                            give(ins) if blk else tell(ins)
                        tell(V.tensor_scalar(fst[:, 1, :, h], fst[:, 0, :, h], -1.0, None, ALU.mult), f_max)
                        if h + 2 < R_H:
                            seg(h + 2)
                    if 1 <= h < R_H + 1:
                        normalise(h - 1)
                    if h >= 4 and h % 2 == 0:
                        b = take()
                        give(V.tensor_copy(foT[:, (h - 4) // 2, :], b[:, 0:256]))

            def rwkv():
                m0 = mark["rwkv"][0]
                rs = r_hid[:, 2, :]
                dve.wait_ge(act_free, mark[("norm", 1, 0)][0] + 2)
                tell(V.memset(rs, 1.0))
                tell(V.memset(rs.rearrange("p (c t) -> p c t", t=CH)[:, :, 0:1], 0.0))
                tell(V.tensor_tensor(r_dx[:, :, 1:S], hT[:, :, 0:S - 1], hT[:, :, 1:S], ALU.subtract))
                tell(V.tensor_scalar(r_dx[:, :, 0:1], hT[:, :, 0:1], -1.0, None, ALU.mult))
                waits = [0, 0, m0 + 1, m0 + 2, m0 + 3, mark[("rkv", 0)][0] + 4]
                for n, (mi, buf) in enumerate(zip((3, 4, 5, 0, 1, 2), (r_xsA, r_xsB) * 3)):
                    if waits[n]:
                        dve.wait_ge(act_full, waits[n])
                    for k in range(KD):
                        tell(V.scalar_tensor_tensor(out=buf[:, k, :], in0=r_dx[:, k, :], scalar=col("r_mix", mi * KD + k),
                                                    in1=hT[:, k, :], op0=ALU.mult, op1=ALU.add), xs_ready if k == KD - 1 else dve_step)
                for j in range(4):
                    b = take()
                    give(V.tensor_copy(flat(r_k[:, 2 * j:2 * j + 2, :]), b[:, :]))
                tell(V.tensor_tensor(r_xsA[:, :, :], r_k[:, :, :], wide("r_k_k", 0), ALU.mult), r_v2a)
                dve.wait_ge(act_free, m0 + 11)
                for k in range(KD):
                    tell(V.tensor_tensor_scan(r_dx[:, k, :], rs, r_s[:, k, :], 0.0, ALU.mult, ALU.add))
                tell(V.tensor_tensor(r_s[:, :, :], r_dx[:, :, :], r_s[:, :, :], ALU.subtract), r_v2a)
                dve.wait_ge(r_a2v, 4)
                tell(V.tensor_scalar(flat(r_xsB), flat(r_xsB), 1e-12, None, ALU.max))
                tell(V.reciprocal(flat(r_xsB), flat(r_xsB)))
                tell(V.tensor_tensor(flat(r_xsA), flat(r_xsA), flat(r_xsB), ALU.mult))
                tell(V.scalar_tensor_tensor(out=r_xsB[:, :, :], in0=r_a[:, :, :], scalar=-1.0, in1=wide("r_k_a", 0), op0=ALU.add, op1=ALU.mult))
                tell(V.scalar_tensor_tensor(out=flat(r_k), in0=flat(r_xsB), scalar=1.0, in1=flat(r_k), op0=ALU.add, op1=ALU.mult), r_v2a)
                dve.wait_ge(r_a2v, 5)
                tell(V.scalar_tensor_tensor(out=flat(r_s), in0=flat(r_xsA), scalar=-1.0, in1=flat(r_s), op0=ALU.mult, op1=ALU.mult))
                tell(V.tensor_tensor(flat(r_xsA), flat(r_xsA), flat(r_a), ALU.mult))
                tell(V.tensor_tensor(flat(r_a), flat(r_r), flat(r_k), ALU.mult))
                tell(V.tensor_tensor(r_a[:, :, :], r_a[:, :, :], wide("r_r_k", 0), ALU.mult), r_v2p)
                dve.wait_ge(r_a2v, 6)
                tell(V.tensor_tensor(flat(r_xsA), flat(r_xsA), flat(r_xsB), ALU.mult))
                tell(V.tensor_tensor(flat(r_k), flat(r_k), flat(r_xsB), ALU.mult))
                dve.wait_ge(r_a2v, 7)
                tell(V.tensor_copy(pend[:, :, :], r_dx[:, :, CH - 1:S:CH]))
                tell(V.tensor_tensor(flat(r_r), flat(r_r), flat(r_dx), ALU.mult), r_v2p)
                for j in range(4):
                    b = take()
                    v = flat(r_v[:, 2 * j:2 * j + 2, :])
                    give(V.tensor_tensor(v, v, b[:, :], ALU.mult))

                def blocks(b):
                    return b[:, :].rearrange("p (c d) -> p c d", c=4)

                def own(v, B, q, pr):
                    return v[pr, 4 * B + q:4 * B + q + 3:2, :, :]

                def diag(src, par):
                    pr = slice(64 * par, 64 * par + 64)
                    return src[pr].rearrange("p (i t) d -> p i t d", i=2)[:, :, :, 64 * par:64 * par + 64]

                def ns(B, q, lv, s=ns_ready):
                    tell(V.tensor_tensor(wk[q][1][:, :, :], wk[q][0][:, :, :], level[:, lv, :].unsqueeze(1).broadcast_to([P, 4, P]), ALU.mult), ns_ready)
                eye = ident[:, :].unsqueeze(1).broadcast_to([P, 4, P])
                for B in range(4):
                    for q in range(2):
                        b = take()
                        give(V.tensor_copy(flat(wk[q][0]), b[:, :]))
                        b = take()
                        for par in range(2):
                            pr = slice(64 * par, 64 * par + 64)
                            ms = upto_c[pr, 64 * par:64 * par + 64].unsqueeze(1).unsqueeze(1).broadcast_to([64, 2, 2, 64])
                            ins = V.tensor_tensor(own(r_Arb, B, q, pr), diag(blocks(b), par), ms, ALU.mult)
                            give(ins) if par else tell(ins)
                        for m, ms in enumerate((before_c, upto_c)):
                            b = take()
                            give(V.tensor_tensor(r_mk[q][m][:, :, :], blocks(b), ms[:, :].unsqueeze(1).broadcast_to([P, 4, P]), ALU.mult))
                    for q in range(2):
                        ns(B, q, 0)
                    for q in range(2):
                        tell(V.tensor_tensor(wk[q][2][:, :, :], wk[q][1][:, :, :], eye, ALU.add))
                    for q in range(2):
                        b = take()
                        give(V.tensor_tensor(wk[q][3][:, :, :], blocks(b), eye, ALU.add))
                        ns(B, q, 1)
                    for lv in range(1, 6):
                        for q in range(2):
                            b = take()
                            if lv < 5:
                                for m in (3, 2):
                                    if m == 2:
                                        b = take()
                                    give(V.tensor_tensor(flat(wk[q][m]), flat(wk[q][m]), b[:, :], ALU.add))
                                ns(B, q, lv + 1)
                            else:
                                if B == 3 and q == 1:
                                    tell(V.memset(r_S[:, :, :], 0.0))
                                for par in range(2):
                                    pr = slice(64 * par, 64 * par + 64)
                                    ins = V.tensor_tensor(own(r_XT4, B, q, pr), diag(wk[q][3], par), diag(blocks(b), par), ALU.add)
                                    give(ins) if par else tell(ins)
                dve.wait_ge(act_free, mark["chunks"][0])
                for c in range(NC):
                    tt, par = c // 2, c % 2
                    pr = slice(64 * par, 64 * par + 64)
                    cs = slice(c * CH, (c + 1) * CH)

                    def heads8(b, r):
                        return b[r, :].rearrange("p (k d) -> p k d", k=KD)
                    for q in range(2):
                        b = take()
                        give(V.tensor_tensor(r_R[pr, q, :, :], heads8(b, pr), r_U[pr, :, tt, 64 * q:64 * q + 64], ALU.add))
                    for q in range(2):
                        b = take()
                        qr = slice(64 * q, 64 * q + 64)
                        give(V.tensor_tensor(r_k[qr, :, cs], r_k[qr, :, cs], heads8(b, qr), ALU.add))
                    b = take()
                    give(V.tensor_tensor(r_k[:, :, cs], r_k[:, :, cs], heads8(b, slice(0, P)), ALU.add))
                    if c < NC - 1:
                        b = take()
                        tell(V.tensor_tensor(flat(r_S), flat(r_S), b[:, :], ALU.add))
                        give(V.tensor_tensor(r_S[:, :, :], r_S[:, :, :], pend[:, :, c:c + 1].broadcast_to([P, KD, HD]), ALU.mult))
                for j in range(4):
                    b = take()
                    v = flat(r_k[:, 2 * j:2 * j + 2, :])
                    give(V.scalar_tensor_tensor(out=v, in0=b[:, :], scalar=-1.0 / HD, in1=v, op0=ALU.mult, op1=ALU.add))
                for j in range(4):
                    dve.wait_ge(r_a2v, 8 + j)
                    v = flat(r_k[:, 2 * j:2 * j + 2, :])
                    tell(V.tensor_tensor(v, v, flat(r_dx[:, 2 * j:2 * j + 2, :]), ALU.mult))
                    for u in range(2):
                        k = 2 * j + u
                        tell(V.tensor_scalar(r_k[:, k, :], r_k[:, k, :], col("r_lnx_w", k), col("r_lnx_b", k), ALU.mult, ALU.add))
                    tell(V.tensor_tensor(v, v, flat(r_v[:, 2 * j:2 * j + 2, :]), ALU.add))
                    b = take()
                    give(V.tensor_tensor(v, v, b[:, :], ALU.mult))

            dve.wait_ge(cond_ready, 1)
            dve.wait_ge(row_landed, 16 * N_ROWS)
            tell(V.tensor_scalar(qkw[:, 0:1], qkw[:, 0:1], HD ** -0.5, None, ALU.mult))
            dve.wait_ge(ada_bias, 16)
            dve.wait_ge(consts, 1)
            for s in range(NADA):
                adaln(0, s)
            modulation(0)
            for l in range(DEPTH):
                norm(l, 0)
                if l % 3 == 0:
                    mamba(l // 3)
                elif l % 3 == 1:
                    rwkv()
                else:
                    fox()
                residual(0)
                norm(l, 1)
                ffn(l)
                if l + 1 < DEPTH:
                    modulation(l + 1)

        @block.scalar
        def _(act):
            A = nc.scalar.activation
            counts = {}
            job = [0]

            def tell(ins, s=act_step):
                counts[s.name] = counts.get(s.name, 0) + 1
                ins.then_inc(s, 1)
                act.wait_ge(s, counts[s.name])

            def take():
                act.wait_ge(act_full, job[0] + 1)
                return psum_act[job[0] % 2]

            def give(ins):
                job[0] += 1
                ins.then_inc(act_free, 1)
                act.wait_ge(act_free, job[0])

            def flat(v):
                return v.rearrange("p a b -> p (a b)")

            def col(name, i):
                return vcol[:, COL[name] + i:COL[name] + i + 1]
            norms = [0]

            def norm(l, which):
                if norms[0] == 0:
                    act.wait_ge(x_landed, 16)
                else:
                    act.wait_ge(acc_free, 4 * norms[0])
                for tt in range(TT):
                    tell(A(xn[:, tt, :], x[:, tt, :], ACT.Square, accum_out=small[:, tt:tt + 1]))
                tell(A(small[:, 2:4], small[:, 0:2], ACT.Ln, scale=1.0 / D, bias=epsc[:, 0:1]))
                tell(A(small[:, 4:6], small[:, 2:4], ACT.Exp, scale=-0.5), rstd_ready)
                act.wait_ge(mod_ready, l + 1)
                for j in (0, 2):
                    b = take()
                    for u in range(2):
                        k = 2 * j + u
                        ins = A(hT[:, k, :], b[:, u * S:(u + 1) * S], ACT.Identity, scale=nsc[:, which, k:k + 1],
                                bias=mcol[:, 16 * which + k:16 * which + k + 1])
                        give(ins) if u else tell(ins)
                norms[0] += 1

            def ffn(l):
                for i in range(KF // 2):
                    b = take()
                    give(A(flat(gT[:, 2 * i:2 * i + 2, :]), b[:, :], ACT.Silu))

            def log1p_exp(v):
                tell(A(v[:, 1], v[:, 0], ACT.Abs))
                tell(A(v[:, 2], v[:, 1], ACT.Exp, scale=-1.0))
                tell(A(v[:, 2], v[:, 2], ACT.Ln, bias=epsc[:, 2:3]), dt_e)

            def mamba(o):
                act.wait_ge(dve_free, mark[("mamba", o)][1] + 1)
                log1p_exp(dtv)
                for j in range(16):
                    act.wait_ge(dve_free, mark[("conv", o)][1] + j + 1)
                    v = flat(xbcT[:, 2 * j:2 * j + 2, :])
                    tell(A(v, v, ACT.Silu), xbc_silu)
                for h in range(M_H):
                    b = take()
                    if h >= 3:
                        act.wait_ge(gmat_ready, M_H * o + h - 2)
                    give(A(dec[:, h % 3, :], b[:, 0:384], ACT.Exp))
                for g in range(M_G + 1):
                    if g < M_G:
                        b = take()
                        if g >= 2:
                            act.wait_ge(yz_ready, M_G * o + g - 1)
                        give(A(zs[:, g % 2, :], b[:, :], ACT.Silu))
                    if g:
                        act.wait_ge(yz_ready, M_G * o + g)
                        tell(A(flat(sqz[:, 2 * g - 2:2 * g, :]), flat(xbcT[:, 2 * g - 2:2 * g, :]), ACT.Square), sq_ready)
                for g in range(M_G):
                    b = take()
                    if g >= 2:
                        act.wait_ge(yn_ready, M_G * o + g - 1)
                    give(A(rsm[:, g % 2, :], b[:, 0:256], ACT.Ln, scale=1.0 / 256, bias=epsc[:, 0:1]))
                    tell(A(rsm[:, g % 2, :], rsm[:, g % 2, :], ACT.Exp, scale=-0.5), rs_ready)

            def fox():
                act.wait_ge(dve_free, mark["fox"][1] + 1)
                log1p_exp(ffv)

                def project(i):
                    b = take()
                    m, j = i // 4, i % 4
                    tell(A(fsq[:, i % 2, :], b[:, :], ACT.Square), f_sq)
                    give(A(flat(fqk[:, m, 2 * j:2 * j + 2, :]), b[:, :], ACT.Copy))

                def inv_rms(i):
                    b = take()
                    if i >= 2:
                        act.wait_ge(f_qk, i - 1)
                    give(A(frs[:, i % 2, :], b[:, :], ACT.Ln, scale=1.0 / HD, bias=epsc[:, 0:1]))
                    tell(A(frs[:, i % 2, :], frs[:, i % 2, :], ACT.Exp, scale=-0.5), f_rs)
                for i in range(8):
                    project(i)
                    if i:
                        inv_rms(i - 1)
                inv_rms(7)
                d0 = mark["foxhead"][1]
                for h in range(R_H + 2):
                    if h < R_H:
                        act.wait_ge(f_max, h + 1)
                        for blk, r in enumerate((slice(0, P), slice(P, 384))):
                            tell(A(flg[:, h % 4, r], flg[:, h % 4, r], ACT.Exp, bias=fst[:, 1, blk, h:h + 1],
                                   accum_out=fst[:, 2, blk, h:h + 1]), f_exp if blk else act_step)
                    if h >= 2:
                        hh = h - 2
                        b = take()
                        if hh >= 4:
                            p = (hh - 4) // 2
                            act.wait_ge(dve_full, d0 + min(2 * p + 5, R_H) + p + 1)
                        give(A(fpT[:, hh % 4, :], b[:, 0:384], ACT.Copy))

            def rwkv():
                b = take()
                give(A(r_hid[0:64, 0, :], b[0:64, 0:S], ACT.Tanh))
                b = take()
                give(A(r_hid[64:128, 0, :], b[64:128, 0:S], ACT.Copy))
                b = take()
                tell(A(r_hgS[:, 0, :], b[:, 0:S], ACT.Sigmoid))
                give(A(r_hgS[0:32, 1, :], b[0:32, S:2 * S], ACT.Sigmoid))
                for m, (dst, w) in enumerate(((r_s, "r_w0"), (r_a, "r_a0"))):
                    for j in range(4):
                        b = take()
                        for u in range(2):
                            k = 2 * j + u
                            ins = A(dst[:, k, :], b[:, u * S:(u + 1) * S], ACT.Sigmoid, bias=col(w, k))
                            give(ins) if u else tell(ins)
                for dst in (r_r, r_v):
                    for j in range(4):
                        b = take()
                        give(A(flat(dst[:, 2 * j:2 * j + 2, :]), b[:, :], ACT.Copy))

                def tokens(dst):
                    for j in range(4):
                        b = take()
                        give(A(dst[:, :, 256 * j:256 * j + 256], b[:, :].rearrange("p (t d) -> p t d", t=TT), ACT.Copy))
                tokens(r_vt)
                act.wait_ge(r_v2a, 1)
                for j in range(4):
                    tell(A(flat(r_xsB[:, 2 * j:2 * j + 2, :]), flat(r_xsA[:, 2 * j:2 * j + 2, :]), ACT.Square), r_a2p)
                for j in range(4):
                    b = take()
                    ins = A(flat(r_xsB[:, 2 * j:2 * j + 2, :]), b[:, :], ACT.Sqrt)
                    give(ins)
                    tell(A(small[:, 6:7], epsc[:, 2:3], ACT.Copy), r_a2v)
                act.wait_ge(r_v2a, 2)
                tell(A(flat(r_s), flat(r_s), ACT.Exp, scale=-E_HALF), r_a2v)
                act.wait_ge(r_v2a, 3)
                tell(A(flat(r_xsB), flat(r_dx), ACT.Exp, scale=E_HALF), r_a2v)
                tell(A(flat(r_dx), flat(r_dx), ACT.Exp, scale=-E_HALF), r_a2v)
                tokens(r_bt)
                tokens(r_kt)
                for B in range(4):
                    for q in range(2):
                        b = take()
                        give(A(r_U[:, 2 * B:2 * B + 2, :, 64 * q:64 * q + 64],
                               b[:, 0:256].rearrange("p (i t d) -> p i t d", i=2, t=2), ACT.Copy))
                        b = take()
                        qr = slice(64 * q, 64 * q + 64)
                        give(A(flat(r_k[qr, 2 * B:2 * B + 2, :]), b[qr, :], ACT.Copy))
                    for lv in range(1, 6):
                        for q in range(2):
                            b = take()
                            give(A(flat(wk[q][4]), b[:, :], ACT.Copy))
                for c in range(NC):
                    pr = slice(64 * (c % 2), 64 * (c % 2) + 64)
                    for q in range(2):
                        b = take()
                        give(A(flat(r_SA[pr, q, :, :]), b[pr, :], ACT.Copy))
                for j in range(4):
                    act.wait_ge(dve_free, mark["gn"][1] + j + 1)
                    tell(A(flat(r_dx[:, 2 * j:2 * j + 2, :]), flat(r_k[:, 2 * j:2 * j + 2, :]), ACT.Square), r_a2p)
                for j in range(4):
                    b = take()
                    v = flat(r_dx[:, 2 * j:2 * j + 2, :])
                    give(A(v, b[:, :], ACT.Ln, scale=1.0 / HD, bias=epsc[:, 1:2]))
                    tell(A(v, v, ACT.Exp, scale=-0.5), r_a2v)

            for v in range(NVT):
                b = take()
                r = min(P, NVEC - v * P)
                give(A(vcol[:, v * P:v * P + r], b[:, 0:r], ACT.Copy))
            act.wait_ge(consts, 1)
            act.wait_ge(row_landed, 16 * N_ROWS)
            tell(A(rowb[:, 64:128], rowb[:, 64:128], ACT.Exp))
            tell(A(vcol[:, 0:KD], vcol[:, 0:KD], ACT.Silu), cond_ready)
            for l in range(DEPTH):
                norm(l, 0)
                if l % 3 == 0:
                    mamba(l // 3)
                elif l % 3 == 1:
                    rwkv()
                else:
                    fox()
                norm(l, 1)
                ffn(l)

        @block.gpsimd
        def _(pool):
            G = nc.gpsimd
            n = [0]

            def done(ins):
                n[0] += 1
                ins.then_inc(pool_step, 1)
                pool.wait_ge(pool_step, n[0])

            def select(v, pattern, base, mult, fill=0.0, op=ALU.is_ge):
                done(G.affine_select(out=v, in_=v, compare_op=op, fill=fill, base=base, pattern=pattern, channel_multiplier=mult))

            for name, r, m, p0, tile in vector_parts():
                src = t[name].rearrange(VEC_LAYOUT[name]).rearrange("(r p) -> r p", p=P)
                pool.dma_start(vrow[p0:p0 + m, tile, :], src[r:r + m, :]).then_inc(vec_landed, 16)
            for i, (dst, src) in enumerate((
                    (rowb[:, 0:64], t["m_dt_bias"].rearrange("a h -> (a h)").partition_broadcast(P)),
                    (rowb[:, 64:128], t["m_A_log"].rearrange("a h -> (a h)").partition_broadcast(P)),
                    (rowb[:, 128:144], t["f_fgate_b"].rearrange("a h -> (a h)").partition_broadcast(P)),
                    (qkw[0:64, 0:1], t["f_q_norm_w"].rearrange("a h -> h a")), (qkw[64:128, 0:1], t["f_q_norm_w"].rearrange("a h -> h a")),
                    (qkw[0:64, 1:2], t["f_k_norm_w"].rearrange("a h -> h a")), (qkw[64:128, 1:2], t["f_k_norm_w"].rearrange("a h -> h a")),
                    (dskip[0:64, :, :].rearrange("p a b -> p (a b)"), t["m_D"].rearrange("a (c two) -> two (a c)", two=2)[0].partition_broadcast(64)),
                    (dskip[64:128, :, :].rearrange("p a b -> p (a b)"), t["m_D"].rearrange("a (c two) -> two (a c)", two=2)[1].partition_broadcast(64)))):
                with nc.allow_non_contiguous_dma(reason="a few columns"):
                    pool.dma_start(dst, src).then_inc(row_landed, 16)
            done(G.memset(ada[:, :], 0.0))
            pool.dma_start(ada[0:1, :], t["ada_b"][0:1, :]).then_inc(ada_bias, 16)
            pool.dma_start(wnar[:, :, :], t["m_in_w"][0][:, M_IN + M_XBC:].rearrange("(k p) n -> p k n", p=P)).then_inc(wdt_landed, 16)
            done(G.memset(ones[:, :], 1.0))
            done(G.memset(ident[:, :], 0.0))
            select(ident[:, :], [[-1, P]], 0, 1, 1.0, ALU.not_equal)
            done(G.memset(halves[:, :], 0.0))
            done(G.memset(halves[0:64, 0:64], 1.0))
            done(G.memset(halves[64:128, 64:128], 1.0))
            done(G.memset(upto[:, :], 1.0))
            select(upto[:, 0:256], [[1, 256]], 0, -1)
            select(upto[:, 256:384], [[1, P]], 0, -1)
            done(G.memset(after[:, :], 1.0))
            select(after[:, :], [[-1, P]], -1, 1)
            done(G.memset(neg[:, :], 0.0))
            select(neg[:, 0:P], [[-1, P]], 0, 1, NEG)
            select(neg[:, 256:384], [[-1, P]], 0, 1, NEG)
            done(G.memset(epsc[:, 0:1], EPS))
            done(G.memset(epsc[:, 1:2], R_GN_EPS))
            done(G.memset(epsc[:, 2:3], 1.0))
            for m, dlt in ((before_c, -1), (upto_c, 0)):
                done(G.tensor_copy(m[:, :], halves[:, :]))
                select(m[:, :], [[1, P]], dlt, -1)
            for lv in range(6):
                s = 1 << lv
                done(G.memset(level[:, lv, :], 0.0))
                v = level[:, lv, :].rearrange("p (b r) -> p b r", r=2 * s)[:, :, 0:s]
                done(G.memset(v, 1.0))
                select(v, [[-2 * s, P // (2 * s)], [0, s]], -s, 1)
                select(v, [[2 * s, P // (2 * s)], [0, s]], 2 * s - 1, -1)
            G.memset(small[:, 6:8], 0.0).then_inc(consts, 1)
            for l in range(1, DEPTH):
                pool.wait_ge(acc_free, 8 * l - 4)
                if l == 1:
                    pool.dma_start(wnar[:, :, 0:R_H], t["f_qkvf_w"][0][:, 3 * D:].rearrange("(k p) n -> p k n", p=P)).then_inc(wdt_landed, 16)
                if l == 3:
                    pool.dma_start(wnar[:, :, :], t["m_in_w"][1][:, M_IN + M_XBC:].rearrange("(k p) n -> p k n", p=P)).then_inc(wdt_landed, 16)
                done(G.memset(ada[:, :], 0.0))
                pool.dma_start(ada[0:1, :], t["ada_b"][l:l + 1, :]).then_inc(ada_bias, 16)

        @block.sync
        def _(sp):
            sp.dma_start(x[:, :, :], t["x"][0].rearrange("(t p) d -> p t d", p=P)).then_inc(x_landed, 16)
            for n, parts in enumerate(loads):
                if n >= RING:
                    sp.wait_ge(*release[n - RING])
                for cols, src, who, w in parts:
                    if isinstance(who, tuple):
                        dst = slot(n)[who[0]:who[1], cols]
                    else:
                        dst = slot(n)[:, cols].rearrange("p (k c) -> p k c", c=w)
                    sp.dma_start(dst, src).then_inc(landed[n % RING], 16)
            sp.wait_ge(acc_free, 8 * DEPTH)
            sp.dma_start(out[0].rearrange("(t p) d -> p t d", p=P), x[:, :, :]).then_inc(out_landed, 16)
            sp.wait_ge(out_landed, 16)


_OUTS = [((1, S, D), 'float32')]


def kernel(**inputs):
    import numpy as _np
    import concourse.bacc as _bacc
    from concourse import mybir as _mybir
    from concourse.bass_utils import run_bass_kernel_spmd as _run

    nc = _bacc.Bacc("TRN2", target_bir_lowering=False, num_devices=1)
    arrays, args = {}, {}
    for name in inputs:
        a = _np.ascontiguousarray(inputs[name])
        arrays[f"in_{name}_dram"] = a
        args[name] = nc.dram_tensor(f"in_{name}_dram", a.shape, _mybir.dt.from_np(a.dtype), kind="ExternalInput").ap()
    outs = []
    for i, (shape, dtype) in enumerate(_OUTS):
        dt = _mybir.dt.from_np(_np.dtype(dtype))
        outs.append(nc.dram_tensor(f"out_{i}_dram", shape, dt, kind="ExternalOutput").ap())
    trunk(nc, args, outs[0])
    r = _run(nc, [arrays], core_ids=[0])
    return r.results[0]["out_0_dram"]
```

```python
from contextlib import ExitStack
import math

import numpy as np
import concourse.bass as bass
from concourse import mybir

ALU = mybir.AluOpType
ACT = mybir.ActivationFunctionType
AX = mybir.AxisListType
F32 = mybir.dt.float32
F32R = mybir.dt.float32r

P = 128
D = 1024
S = 256
DEPTH = 4
KD = D // P
TT = S // P
NB = 512
DFF = 2816
KF = DFF // P
M_IN = 2048
M_KT = M_IN // P
M_XBC = 4096
M_G = 8
M_H = 32
HD = 64
R_H = 16
LORA = 64
LORA_G = 160
CH = 64
NC = S // CH
EPS = 1e-6
R_GN_EPS = 64e-5
E_HALF = math.exp(-0.5)
UNIT = 1024
SLOT = 2 * UNIT
RING = 3
UNITS = 5
NADA = 24
NEG = -1e30

VECTORS = [("c", KD), ("norm1_w", 4 * KD), ("norm2_w", 4 * KD), ("m_conv_w", 256), ("m_conv_b", 64),
           ("m_norm_w", 32), ("r_mix", 48), ("r_w0", 8), ("r_a0", 8), ("r_k_k", 8), ("r_k_a", 8),
           ("r_r_k", 8), ("r_lnx_w", 8), ("r_lnx_b", 8)]
COL = {}
_at = 0
for _n, _r in VECTORS:
    COL[_n] = _at
    _at += _r
NVEC = _at
NVT = -(-NVEC // P)


N_ROWS = 9
VEC_LAYOUT = {"c": "a d -> (a d)", "norm1_w": "a d -> (a d)", "norm2_w": "a d -> (a d)", "m_conv_w": "a b d -> (a b d)",
              "m_conv_b": "a d -> (a d)", "m_norm_w": "a d -> (a d)", "r_mix": "a b d -> (a b d)", "r_r_k": "a b d -> (a b d)"}
for _n in ("r_w0", "r_a0", "r_k_k", "r_k_a", "r_lnx_w", "r_lnx_b"):
    VEC_LAYOUT[_n] = "a d -> (a d)"


def vector_parts():
    out = []
    for name, n in VECTORS:
        r = 0
        while r < n:
            at = COL[name] + r
            m = min(n - r, P - at % P)
            out.append((name, r, m, at % P, at // P))
            r += m
    return out


def trunk(nc, t, out):
    with ExitStack() as ctx:
        def sb(name, shape):
            return ctx.enter_context(nc.sbuf_tensor(name, shape, F32))

        def sem(name):
            return ctx.enter_context(nc.semaphore(name))

        base = -(-nc.sbuf_base // 32) * 32
        ARENA = 25600
        arena = sb("arena", [P, ARENA])
        hT = sb("hT", [P, KD, S])
        assert nc.sbuf_base == base + 4 * (ARENA + KD * S)

        def part(name, off, *shape):
            return nc.alloc_sbuf_tensor_at(name, [P, *shape], F32R, offset=base + 4 * off)
        x = sb("x", [P, TT, D])
        ring = sb("ring", [P, RING, SLOT])
        gate = sb("gate", [P, 2, D])
        vcol = sb("vcol", [P, NVEC])
        mcol = sb("mcol", [P, 32])
        nsc = sb("nsc", [P, 2, KD])
        ident = sb("ident", [P, P])
        ones = sb("ones", [P, P])
        halves = sb("halves", [P, P])
        upto = sb("upto", [P, 384])
        after = sb("after", [P, P])
        neg = sb("neg", [P, 384])
        level = sb("level", [P, 6, P])
        before_c = sb("before_c", [P, P])
        upto_c = sb("upto_c", [P, P])
        wnar = sb("wnar", [P, KD, M_H])
        small = sb("small", [P, 8])
        epsc = sb("epsc", [P, 3])
        dskip = sb("dskip", [P, 2, M_KT])
        qkw = sb("qkw", [P, 2])
        rowb = sb("rowb", [P, 160])
        pend = sb("pend", [P, KD, NC])
        w_hi = ctx.enter_context(nc.sbuf_tensor("w_hi", [P, UNITS, UNIT], F32R))
        w_lo = ctx.enter_context(nc.sbuf_tensor("w_lo", [P, UNITS, UNIT], F32R))
        wn_hi = ctx.enter_context(nc.sbuf_tensor("wn_hi", [P, KD, M_H], F32R))
        wn_lo = ctx.enter_context(nc.sbuf_tensor("wn_lo", [P, KD, M_H], F32R))
        h_hi2 = (part("h_hi_mixer", 18880, KD, S), part("h_hi_ffn", 14848, KD, S))
        h_lo = part("h_lo", ARENA, KD, S)
        g_hi = part("g_hi", 2048, KF, S)
        g_lo = part("g_lo", 7680, KF, S)
        y_hi = part("y_hi", 4096, M_KT, S)
        y_lo = part("y_lo", 0, M_KT, S)
        o_hi = part("o_hi", 6144, KD, S)
        o_lo = part("o_lo", 14592, KD, S)
        psum_acc = [ctx.enter_context(nc.psum_tensor(f"psum_acc{i}", [P, NB], F32)) for i in range(4)]
        psum_act = [ctx.enter_context(nc.psum_tensor(f"psum_act{i}", [P, NB], F32)) for i in range(2)]
        psum_dve = [ctx.enter_context(nc.psum_tensor(f"psum_dve{i}", [P, NB], F32)) for i in range(2)]

        def carve(off, *dims):
            n = int(np.prod(dims))
            assert off + n <= ARENA, (off, n)
            v = arena[:, off:off + n]
            if len(dims) == 2:
                v = v.rearrange("p (a b) -> p a b", a=dims[0])
            elif len(dims) == 3:
                v = v.rearrange("p (a b c) -> p a b c", a=dims[0], b=dims[1])
            elif len(dims) == 4:
                v = v.rearrange("p (a b c d) -> p a b c d", a=dims[0], b=dims[1], c=dims[2])
            return v

        vrow = carve(8192, NVT, P)
        xn = carve(0, TT, D)
        gx = carve(13312, 3, NB)
        ada = carve(ARENA - 6144, 6144)
        xbcT = carve(0, 32, S)
        xd = carve(8192, TT, M_IN)
        sqz = carve(8192, M_KT, S)
        scT = carve(12288, M_G, 384)
        dec = carve(15360, 3, 384)
        gm = carve(16512, 4, 384)
        segw = carve(18048, 2, 2, P)
        zs = carve(15360, 2, NB)
        rsm = carve(16512, 2, S)
        dtv = carve(18560, 5, TT, M_H)
        fqk = carve(0, 2, KD, S)
        fv = carve(4096, TT, D)
        fsq = carve(8192, 2, NB)
        frs = carve(9216, 2, NB)
        fsegw = carve(10240, 2, 384)
        flg = carve(11008, 4, 384)
        fpT = carve(12544, 4, 384)
        fst = carve(14080, 4, 2, R_H)
        ffv = carve(14208, 5, TT, R_H)
        A8 = [carve(2048 * i, KD, S) for i in range(8)]
        r_dx, r_xsA, r_xsB, r_s, r_a, r_r, r_k, r_v = A8
        r_XT = carve(16384, 32, HD)
        wk = [[carve(18432 + 2560 * q + 512 * i, 4, P) for i in range(5)] for q in range(2)]
        r_mk = [[carve(23552 + 1024 * q + 512 * i, 4, P) for i in range(2)] for q in range(2)]
        r_R = carve(23552, 2, KD, HD)
        r_SA = carve(24576, 2, KD, HD)
        r_hid = carve(18432, 3, S)
        r_vt = hT[:, :, :].rearrange("p a b -> p (a b)").rearrange("p (t d) -> p t d", t=TT)
        r_bt = arena[:, 0:2048].rearrange("p (t d) -> p t d", t=TT)
        r_kt = arena[:, 4096:6144].rearrange("p (t d) -> p t d", t=TT)
        r_U = arena[:, 2048:4096].rearrange("p (k t d) -> p k t d", k=KD, t=TT)
        r_Arb = arena[:, 8192:10240].rearrange("p (h t d) -> p h t d", h=R_H, t=TT)
        r_XT4 = arena[:, 16384:18432].rearrange("p (h t d) -> p h t d", h=R_H, t=TT)
        r_S = carve(18432, KD, HD)
        r_xsR, r_xsV = carve(19456, KD, S), carve(21504, KD, S)
        r_hgS = sb("r_hgS", [P, 2, S])

        act_full, act_free = sem("act_bank_full"), sem("act_bank_free")
        dve_full, dve_free = sem("dve_bank_full"), sem("dve_bank_free")
        acc_full, acc_free = sem("acc_full"), sem("acc_free")
        act_step, dve_step, pool_step = sem("act_step"), sem("dve_step"), sem("pool_step")
        landed = [sem(f"slot_landed{i}") for i in range(RING)]
        ada_used, unit_used, raw_used = sem("ada_slot_used"), sem("unit_used"), sem("raw_slot_used")
        hi_ready, split_ready = sem("unit_hi_ready"), sem("unit_split_ready")
        h_hi_ready, h_split, g_hi_ready, g_split = sem("h_hi_ready"), sem("h_split"), sem("g_hi_ready"), sem("g_split")
        ident_ready = sem("identity_ready")
        wn_split = sem("narrow_weight_split")
        ada_zero, ada_bias = sem("ada_zeroed"), sem("ada_bias_landed")
        consts, vec_landed, x_landed, row_landed = sem("consts"), sem("vectors_landed"), sem("x_landed"), sem("rows_landed")
        cond_ready, mod_ready = sem("cond_ready"), sem("mod_ready")
        x_ready, rstd_ready, xn_ready = sem("x_ready"), sem("rstd_ready"), sem("xn_ready")
        wdt_landed = sem("narrow_weight_landed")
        dt_e = sem("dt_e")
        xbc_silu, seg_ready, a_ready, gmat_ready = sem("xbc_silu"), sem("seg_ready"), sem("log_decay_ready"), sem("gmat_ready")
        z_ready, yz_ready, sq_ready, rs_ready, yn_ready = (sem("z_ready"), sem("yz_ready"), sem("sq_ready"),
                                                          sem("rs_ready"), sem("yn_ready"))
        yn_done = sem("yn_done")
        f_sq, f_rs, f_qk = sem("fox_sq"), sem("fox_rs"), sem("fox_qk_ready")
        f_max, f_exp, f_norm = sem("fox_max"), sem("fox_exp"), sem("fox_norm")
        xs_ready = sem("rwkv_xs_ready")
        r_v2a, r_a2v = sem("rwkv_dve_to_act"), sem("rwkv_act_to_dve")
        r_v2p, r_a2p, ns_ready = sem("rwkv_dve_to_pe"), sem("rwkv_act_to_pe"), sem("rwkv_ns_ready")
        out_landed = sem("out_landed")
        block = ctx.enter_context(nc.Block())

        loads, key_of = [], {}

        def add(key, *parts):
            key_of[key] = len(loads)
            loads.append(parts)

        def slot(n):
            return ring[:, n % RING, :]

        def rows(w, n0, nn):
            return w[:, n0:n0 + nn].rearrange("(k p) n -> p k n", p=P)

        unit_of, n_units = {}, [0]

        def split(key, *parts):
            add(key, *parts)
            unit_of[key_of[key]] = n_units[0]
            n_units[0] += 2

        def load_ada(l, i):
            m, k = divmod(i, 4)
            add(("ada", l, i), (slice(0, SLOT), t["ada_w"][l][256 * k:256 * k + 256, m * D:(m + 1) * D].rearrange(
                "(k p) n -> p k n", p=P), P, D))

        def load_cols(how, key, w, n0):
            how(key, (slice(0, SLOT), rows(w, n0, 256), P, 256))

        def load_down(how, key, w, i):
            how((*key, i), (slice(0, SLOT), w[256 * i:256 * i + 256, :].rearrange("(k p) n -> p k n", p=P), P, D))

        def load_ffn(l):
            pending = list(range(NADA)) if l + 1 < DEPTH else []
            for i in range(KF // 2):
                for m, w in enumerate(("ffn_w1", "ffn_w3")):
                    load_cols(split, ("up", l, i, m), t[w][l], i * 256)
                    if pending and i and not (m and i % 4 == 3):
                        load_ada(l + 1, pending.pop(0))
            for i in range(KF // 2):
                load_down(split, ("down2", l), t["ffn_w2"][l], i)
                if pending:
                    load_ada(l + 1, pending.pop(0))

        for i in range(8):
            load_ada(0, i)
        for l in range(DEPTH):
            if l % 3 == 0:
                o = l // 3
                for i in range(16):
                    load_cols(split, ("xbc", o, i), t["m_in_w"][o], M_IN + i * 256)
                for i in range(8):
                    load_cols(split, ("z", o, i), t["m_in_w"][o], i * 256)
                    if l == 0:
                        load_ada(0, 8 + i)
                for i in range(8):
                    load_down(split, ("mout", o), t["m_out_w"][o], i)
                    if l == 0:
                        load_ada(0, 16 + i)
            elif l % 3 == 1:
                add(("lora",), (slice(0, 512), rows(t["r_w1"][0], 0, LORA), P, LORA),
                    (slice(512, 1024), rows(t["r_a1"][0], 0, LORA), P, LORA),
                    (slice(1024, 2048), t["r_w2"][0], (0, 64), 0),
                    (slice(1024, 2048), t["r_a2"][0], (64, 128), 0))
                add(("g1",), (slice(0, 1280), rows(t["r_g1"][0], 0, LORA_G), P, LORA_G))
                for j in (1, 0, 2):
                    for i in range(4):
                        load_cols(add, ("rkv", j, i), t["r_w_rkv"][0, j], i * 256)
                add(("g2",), (slice(0, 1024), t["r_g2"][0, 0:128], (0, 128), 0),
                    (slice(1024, 2048), t["r_g2"][0, 128:160], (0, 32), 0))
                for i in range(4):
                    load_down(add, ("rout",), t["r_out_w"][0], i)
            else:
                for i in range(12):
                    load_cols(split, ("qkv", i), t["f_qkvf_w"][0], i * 256)
                for i in range(4):
                    load_down(split, ("fout",), t["f_out_w"][0], i)
            load_ffn(l)

        def unit_view(n, u):
            if loads[n][0][3] == 256:
                return slot(n).rearrange("p (k c) -> p k c", k=KD)[:, :, u * P:(u + 1) * P]
            return slot(n)[:, u * UNIT:(u + 1) * UNIT]

        def first_unit(*key):
            return unit_of[key_of[key]]
        before_rwkv = first_unit("down2", 0, KF // 2 - 1) + 2

        arrive_at, total = [], [0] * RING
        for n, parts in enumerate(loads):
            total[n % RING] += 16 * len(parts)
            arrive_at.append(total[n % RING])
        n_vec_dmas = len(vector_parts())
        release = {}
        unit_release = []
        mark = {}

        def arrive(eng, key):
            n = key_of[key]
            eng.wait_ge(landed[n % RING], arrive_at[n])
            return n

        @block.tensor
        def _(pe):
            jobs = {"act": 0, "dve": 0}

            def open_bank(who):
                n = jobs[who]
                if n >= 2:
                    pe.wait_ge(act_free if who == "act" else dve_free, n - 1)
                return (psum_act if who == "act" else psum_dve)[n % 2]

            def close_bank(who, last):
                jobs[who] += 1
                last.then_inc(act_full if who == "act" else dve_full, 1)
                return jobs[who]

            def note(name):
                mark[name] = (jobs["act"], jobs["dve"])

            def read_out(who, n):
                pe.wait_ge(act_free if who == "act" else dve_free, n)

            def all_read_out():
                if jobs["act"]:
                    pe.wait_ge(act_free, jobs["act"])
                if jobs["dve"]:
                    pe.wait_ge(dve_free, jobs["dve"])

            def mm(o, l, r, start=True, stop=True):
                return nc.tensor.matmul(o, l, r, start=start, stop=stop, skip_group_check=True)

            def tr(o, i, n=P):
                return nc.tensor.transpose(o, i, ident[0:n, 0:n])

            def freed(key, who):
                release[key_of[key]] = ({"act": act_full, "dve": dve_full}[who], jobs[who])

            def mm3(o, l, r, start=True, stop=True):
                mm(o, l[0], r[0], start, False)
                mm(o, l[0], r[1], False, False)
                return mm(o, l[1], r[0], False, stop)

            count = {"which": 0, "unit": 0, "unit_used": 0, "raw": 0, "down": 0}

            def next_unit():
                u = count["unit"]
                count["unit"] += 1
                pe.wait_ge(split_ready, u + 1)
                return w_hi[:, u % UNITS, :], w_lo[:, u % UNITS, :]

            def unit_read(last):
                count["unit_used"] += 1
                last.then_inc(unit_used, 1)
                unit_release.append((unit_used, count["unit_used"]))

            def bank_read(who):
                unit_release.append(({"act": act_full, "dve": dve_full}[who], jobs[who]))

            def down(key, nk, lhs, ready=None, splits=True):
                d = count["down"]
                count["down"] += 1
                if d:
                    pe.wait_ge(acc_free, 4 * d)
                for k in range(nk):
                    if ready:
                        ready(k)
                    if splits:
                        w = next_unit()
                    elif k % 2 == 0:
                        n = arrive(pe, (*key, k // 2))
                    for tt in range(TT):
                        for nh in range(2):
                            o, ns = psum_acc[tt * 2 + nh][:, :], slice(nh * NB, (nh + 1) * NB)
                            if splits:
                                last = mm3(o, lhs(k, tt), (w[0][:, ns], w[1][:, ns]), k == 0, k == nk - 1)
                            else:
                                last = mm(o, lhs(k, tt), slot(n)[:, (k % 2) * D:(k % 2 + 1) * D][:, ns], k == 0, k == nk - 1)
                            if k == nk - 1:
                                last.then_inc(acc_full, 1)
                    if splits:
                        if k < nk - 1:
                            unit_read(last)
                        else:
                            unit_release.append((acc_full, 4 * d + 4))
                    elif k == nk - 1:
                        release[n] = (acc_full, 4 * d + 4)
                    elif k % 2:
                        count["raw"] += 1
                        last.then_inc(raw_used, 1)
                        release[n] = (raw_used, count["raw"])

            def h_parts(k, r=slice(0, S)):
                return h_hi2[count["which"]][:, k, r], h_lo[:, k, r]

            def two_tiles(who):
                b = open_bank(who)
                for u in range(2):
                    w = [v.rearrange("p (k c) -> p k c", k=KD) for v in next_unit()]
                    for k in range(KD):
                        last = mm3(b[:, u * S:(u + 1) * S], (w[0][:, k, :], w[1][:, k, :]), h_parts(k), k == 0, k == KD - 1)
                    if u == 0:
                        unit_read(last)
                close_bank(who, last)
                bank_read(who)

            def two_tiles_raw(key, who, src):
                n = arrive(pe, key)
                w = slot(n).rearrange("p (k c) -> p k c", k=KD)
                b = open_bank(who)
                for u in range(2):
                    for k in range(KD):
                        last = mm(b[:, u * S:(u + 1) * S], w[:, k, u * P:(u + 1) * P], src[:, k, :], k == 0, k == KD - 1)
                close_bank(who, last)
                freed(key, who)

            def narrow(width):
                b = open_bank("dve")
                for tt in range(TT):
                    for k in range(KD):
                        last = mm3(b[:, tt * width:(tt + 1) * width], h_parts(k, slice(tt * P, (tt + 1) * P)),
                                   (wn_hi[:, k, 0:width], wn_lo[:, k, 0:width]), k == 0, k == KD - 1)
                close_bank("dve", last)

            def columns(pieces):
                b = open_bank("dve")
                for j, m in enumerate(pieces):
                    for k in range(KD):
                        last = mm(b[:, j * KD + k:j * KD + k + 1], ada[:, m * D + k * P:m * D + (k + 1) * P], ones[:, 0:1])
                close_bank("dve", last)

            def modulation_a(l):
                pe.wait_ge(ada_used, NADA * l + 8)
                columns((0, 1))

            def modulation_b(l):
                pe.wait_ge(ada_used, NADA * (l + 1))
                for m in (2, 5):
                    for nh in range(2):
                        b = open_bank("dve")
                        close_bank("dve", mm(b[:, :], ones[:, :], ada[:, m * D + nh * NB:m * D + (nh + 1) * NB]))
                columns((3, 4))

            norms = [0]

            def norm(l, which):
                note(("norm", l, which))
                for j in range(4):
                    who = ("act", "dve")[j % 2]
                    b = open_bank(who)
                    for u in range(2):
                        for tt in range(TT):
                            if j == 0 and u == 0:
                                pe.wait_ge(xn_ready, 2 * norms[0] + tt + 1)
                            last = tr(b[:, (2 * u + tt) * P:(2 * u + tt + 1) * P], xn[:, tt, (2 * j + u) * P:(2 * j + u + 1) * P])
                    close_bank(who, last)
                norms[0] += 1
                count["which"] = which
                if (l, which) == (1, 0):
                    all_read_out()
                else:
                    count["split norms"] = count.get("split norms", 0) + 1
                    pe.wait_ge(h_split, 4 * count["split norms"])

            def ffn(l):
                note(("ffn", l))
                for i in range(KF // 2):
                    two_tiles("act")
                    two_tiles("dve")
                down(("down2", l), KF, lambda k, tt: (g_hi[:, k, tt * P:(tt + 1) * P], g_lo[:, k, tt * P:(tt + 1) * P]),
                     lambda k: pe.wait_ge(g_split, KF // 2 * l + k // 2 + 1))

            def mamba(o):
                note(("mamba", o))
                pe.wait_ge(wn_split, 1 if o == 0 else 3)
                narrow(M_H)
                note(("conv", o))
                for i in range(16):
                    two_tiles("dve")
                note(("xT", o))
                pe.wait_ge(xbc_silu, 16 * o + 8)
                for j in range(8):
                    b = open_bank("dve")
                    for tt in range(TT):
                        for u in range(2):
                            last = tr(b[:, (2 * tt + u) * P:(2 * tt + u + 1) * P], xbcT[:, 2 * j + u, tt * P:(tt + 1) * P])
                    close_bank("dve", last)
                note(("score", o))
                pe.wait_ge(xbc_silu, 16 * o + 16)
                for g in range(M_G):
                    b = open_bank("dve")
                    mm(b[:, 0:256], xbcT[:, 16 + g, 0:P], xbcT[:, 24 + g, :])
                    close_bank("dve", mm(b[:, 256:384], xbcT[:, 16 + g, P:S], xbcT[:, 24 + g, P:S]))
                note(("head", o))
                for h in range(M_H + 4):
                    if h < M_H:
                        pe.wait_ge(seg_ready, (M_H + R_H) * o + h + 1)
                        b = open_bank("act")
                        mm(b[:, 0:256], segw[:, h % 2, 0, :], upto[:, 0:256], True, False)
                        mm(b[:, 128:256], dtv[:, 4, 1, h:h + 1].broadcast_to([P, P]), upto[:, 0:P], False, True)
                        close_bank("act", mm(b[:, 256:384], segw[:, h % 2, 1, :], upto[:, 0:P]))
                    if h >= 4 and h % 2 == 0:
                        p = (h - 4) // 2
                        pe.wait_ge(gmat_ready, M_H * o + 2 * p + 2)
                        b = open_bank("dve")
                        for q in range(2):
                            hh, oo = 2 * p + q, slice(HD * q, HD * q + HD)
                            mm(b[oo, 0:256], xd[:, 0, hh * HD:(hh + 1) * HD], gm[:, hh % 4, 0:256], True, False)
                            last = mm(b[oo, 128:256], xd[:, 1, hh * HD:(hh + 1) * HD], gm[:, hh % 4, 256:384], False, True)
                        close_bank("dve", last)
                note(("z", o))
                for i in range(8):
                    two_tiles("act")
                note(("ssum", o))
                for g in range(M_G):
                    pe.wait_ge(sq_ready, M_G * o + g + 1)
                    b = open_bank("act")
                    mm(b[:, 0:256], ones[:, :], sqz[:, 2 * g, :], True, False)
                    close_bank("act", mm(b[:, 0:256], ones[:, :], sqz[:, 2 * g + 1, :], False, True))
                down(("mout", o), M_KT, lambda k, tt: (y_hi[:, k, tt * P:(tt + 1) * P], y_lo[:, k, tt * P:(tt + 1) * P]),
                     lambda k: pe.wait_ge(yn_ready, M_G * o + k // 2 + 1))

            def fox():
                note("fox")
                pe.wait_ge(wn_split, 2)
                narrow(R_H)

                def head_sums(j):
                    pe.wait_ge(f_sq, j + 1)
                    b = open_bank("act")
                    close_bank("act", mm(b[:, :], halves[:, :], fsq[:, j % 2, :]))
                for i in range(8):
                    two_tiles("act")
                    if i:
                        head_sums(i - 1)
                head_sums(7)
                for i in range(4):
                    b = open_bank("dve")
                    for u in range(2):
                        w = [v.rearrange("p (k c) -> p k c", k=KD) for v in next_unit()]
                        for tt in range(TT):
                            for k in range(KD):
                                last = mm3(b[:, tt * 256 + u * P:tt * 256 + (u + 1) * P], h_parts(k, slice(tt * P, (tt + 1) * P)),
                                           (w[0][:, k, :], w[1][:, k, :]), k == 0, k == KD - 1)
                        if u == 0:
                            unit_read(last)
                    close_bank("dve", last)
                    bank_read("dve")
                note("foxhead")
                pe.wait_ge(f_qk, 8)
                for h in range(R_H + 4):
                    if h < R_H:
                        t8, r0 = h // 2, HD * (h % 2)
                        rr = slice(r0, r0 + HD)
                        pe.wait_ge(seg_ready, M_H + h + 1)
                        b = open_bank("dve")
                        sw = fsegw[:, h % 2, :]
                        mm(b[:, 0:P], upto[:, 0:P], sw[:, 0:P], True, False)
                        mm(b[:, 0:P], fqk[rr, 0, t8, 0:P], fqk[rr, 1, t8, 0:P], False, True)
                        mm(b[:, P:384], upto[:, 0:P], sw[:, P:384], True, False)
                        mm(b[:, P:2 * P], ones[:, :], sw[:, 0:P], False, False)
                        close_bank("dve", mm(b[:, P:384], fqk[rr, 0, t8, P:S], fqk[rr, 1, t8, :], False, True))
                    if 2 <= h < R_H + 2:
                        hh = h - 2
                        pe.wait_ge(f_norm, hh + 1)
                        b = open_bank("act")
                        for c in range(3):
                            last = tr(b[:, c * P:(c + 1) * P], flg[:, hh % 4, c * P:(c + 1) * P])
                        close_bank("act", last)
                    if h >= 4 and h % 2 == 0:
                        p = (h - 4) // 2
                        read_out("act", mark["foxhead"][0] + 2 * p + 2)
                        b = open_bank("dve")
                        for q in range(2):
                            hh, oo = 2 * p + q, slice(HD * q, HD * q + HD)
                            mm(b[oo, 0:256], fv[:, 0, hh * HD:(hh + 1) * HD], fpT[:, hh % 4, 0:256], True, False)
                            last = mm(b[oo, P:256], fv[:, 1, hh * HD:(hh + 1) * HD], fpT[:, hh % 4, 256:384], False, True)
                        close_bank("dve", last)
                all_read_out()
                down(("fout",), KD, lambda k, tt: (o_hi[:, k, tt * P:(tt + 1) * P], o_lo[:, k, tt * P:(tt + 1) * P]))

            def rwkv():
                note("rwkv")
                n = arrive(pe, ("lora",))
                w1 = slot(n)[:, 0:512].rearrange("p (k c) -> p k c", k=KD)
                a1 = slot(n)[:, 512:1024].rearrange("p (k c) -> p k c", k=KD)
                w2 = slot(n)[:, 1024:2048]
                pe.wait_ge(xs_ready, 1)
                b = open_bank("act")
                for k in range(KD):
                    last = mm(b[0:64, 0:S], w1[:, k, :], r_xsA[:, k, :], k == 0, k == KD - 1)
                close_bank("act", last)
                pe.wait_ge(xs_ready, 2)
                b = open_bank("act")
                for k in range(KD):
                    last = mm(b[64:128, 0:S], a1[:, k, :], r_xsB[:, k, :], k == 0, k == KD - 1)
                close_bank("act", last)
                pe.wait_ge(xs_ready, 3)
                g1 = slot(arrive(pe, ("g1",)))[:, 0:1280].rearrange("p (k c) -> p k c", k=KD)
                b = open_bank("act")
                for k in range(KD):
                    mm(b[:, 0:S], g1[:, k, 0:P], r_xsA[:, k, :], k == 0, k == KD - 1)
                for k in range(KD):
                    last = mm(b[0:32, S:2 * S], g1[:, k, P:LORA_G], r_xsA[:, k, :], k == 0, k == KD - 1)
                close_bank("act", last)
                freed(("g1",), "act")
                read_out("act", mark["rwkv"][0] + 2)
                for m in range(2):
                    pr = slice(64 * m, 64 * m + 64)
                    for j in range(4):
                        b = open_bank("act")
                        for u in range(2):
                            c = (2 * j + u) * P
                            last = mm(b[:, u * S:(u + 1) * S], w2[pr, c:c + P], r_hid[pr, 0, :])
                        close_bank("act", last)
                freed(("lora",), "act")
                note("kproj")
                pe.wait_ge(xs_ready, 4)
                for i in range(4):
                    two_tiles_raw(("rkv", 1, i), "dve", r_xsB)
                pe.wait_ge(xs_ready, 5)
                for i in range(4):
                    two_tiles_raw(("rkv", 0, i), "act", r_xsR)
                    if i != 1:
                        continue
                    for j in range(4):
                        pe.wait_ge(r_a2p, j + 1)
                        b = open_bank("act")
                        close_bank("act", mm(b[:, :], halves[:, :], arena[:, 4096 + NB * j:4096 + NB * (j + 1)]))
                pe.wait_ge(xs_ready, 6)
                for i in range(4):
                    two_tiles_raw(("rkv", 2, i), "act", r_xsV)
                note("vt")
                read_out("act", mark["vt"][0])
                for j in range(4):
                    b = open_bank("act")
                    for tt in range(TT):
                        for u in range(2):
                            last = tr(b[:, (2 * tt + u) * P:(2 * tt + u + 1) * P], r_v[:, 2 * j + u, tt * P:(tt + 1) * P])
                    close_bank("act", last)
                note("bonus")
                pe.wait_ge(r_v2p, 1)
                for j in range(4):
                    b = open_bank("dve")
                    close_bank("dve", mm(b[:, :], halves[:, :], arena[:, 8192 + NB * j:8192 + NB * (j + 1)]))
                note("bkt")
                pe.wait_ge(r_v2p, 2)
                for src in (r_xsA, r_k):
                    for j in range(4):
                        b = open_bank("act")
                        for tt in range(TT):
                            for u in range(2):
                                last = tr(b[:, (2 * tt + u) * P:(2 * tt + u + 1) * P], src[:, 2 * j + u, tt * P:(tt + 1) * P])
                        close_bank("act", last)
                note("grams")
                KKd, Bi, Ki, Rd = r_s, r_xsA, r_k, r_r
                for B in range(4):
                    def gram(q, lh, rh):
                        pr = slice(64 * q, 64 * q + 64)
                        b = open_bank("dve")
                        for i in range(2):
                            for tt in range(TT):
                                ts = slice(tt * P, (tt + 1) * P)
                                last = mm(b[:, (2 * i + tt) * P:(2 * i + tt + 1) * P], lh[pr, 2 * B + i, ts], rh[pr, 2 * B + i, ts])
                        return close_bank("dve", last)
                    gr = {}
                    for q in range(2):
                        gr[q] = [gram(q, KKd, Bi), gram(q, Bi, Rd), gram(q, Ki, KKd), gram(q, Ki, Rd)]
                    for q in range(2):
                        read_out("dve", gr[q][2])
                        b = open_bank("act")
                        for i in range(2):
                            for tt in range(TT):
                                h = 2 * (2 * B + i) + q
                                last = mm(b[:, (2 * i + tt) * HD:(2 * i + tt + 1) * HD], r_mk[q][0][:, 2 * i + tt, :],
                                          r_vt[:, tt, h * HD:(h + 1) * HD])
                        close_bank("act", last)
                        read_out("dve", gr[q][3])
                        b = open_bank("act")
                        for i in range(2):
                            for tt in range(TT):
                                h = 2 * (2 * B + i) + q
                                last = mm(b[64 * q:64 * q + 64, (2 * i + tt) * P:(2 * i + tt + 1) * P],
                                          r_vt[:, tt, h * HD:(h + 1) * HD], r_mk[q][1][:, 2 * i + tt, :])
                        close_bank("act", last)
                    zr = {}
                    for q in range(2):
                        N_, Ns, X_, Z_, P_ = wk[q]
                        pe.wait_ge(ns_ready, 12 * B + q + 1)
                        b = open_bank("dve")
                        for c in range(4):
                            last = tr(b[:, c * P:(c + 1) * P], Ns[:, c, :])
                        zr[q] = close_bank("dve", last)
                    for lv in range(1, 6):
                        pj = {}
                        for q in range(2):
                            N_, Ns, X_, Z_, P_ = wk[q]
                            pe.wait_ge(ns_ready, 12 * B + 2 * lv + q + 1)
                            read_out("dve", zr[q])
                            b = open_bank("act")
                            for c in range(4):
                                last = mm(b[:, c * P:(c + 1) * P], Ns[:, c, :], Z_[:, c, :])
                            pj[q] = close_bank("act", last)
                        for q in range(2):
                            N_, Ns, X_, Z_, P_ = wk[q]
                            read_out("act", pj[q])
                            b = open_bank("dve")
                            for c in range(4):
                                last = mm(b[:, c * P:(c + 1) * P], X_[:, c, :], P_[:, c, :])
                            zr[q] = close_bank("dve", last)
                            if lv < 5:
                                b = open_bank("dve")
                                for c in range(4):
                                    last = mm(b[:, c * P:(c + 1) * P], P_[:, c, :], X_[:, c, :])
                                zr[q] = close_bank("dve", last)
                note("chunks")
                all_read_out()
                for c in range(NC):
                    tt, par = c // 2, c % 2
                    pr = slice(64 * par, 64 * par + 64)
                    cs = slice(c * CH, (c + 1) * CH)
                    if c:
                        read_out("dve", jobs["dve"])
                    for q in range(2):
                        qr = slice(64 * q, 64 * q + 64)
                        b = open_bank("dve")
                        for k in range(KD):
                            last = mm(b[pr, k * HD:(k + 1) * HD], KKd[qr, k, cs], r_S[qr, k, :])
                        close_bank("dve", last)
                    rj = jobs["dve"]
                    for q in range(2):
                        qr = slice(64 * q, 64 * q + 64)
                        b = open_bank("dve")
                        for k in range(KD):
                            last = mm(b[qr, k * HD:(k + 1) * HD], r_S[qr, k, :], Rd[qr, k, cs])
                        close_bank("dve", last)
                    read_out("dve", rj)
                    for q in range(2):
                        b = open_bank("act")
                        for k in range(KD):
                            last = mm(b[pr, k * HD:(k + 1) * HD], r_XT4[pr, 2 * k + q, tt, :], r_R[pr, q, k, :])
                        close_bank("act", last)
                    read_out("act", jobs["act"])
                    b = open_bank("dve")
                    for k in range(KD):
                        for q in range(2):
                            last = mm(b[64 * q:64 * q + 64, k * HD:(k + 1) * HD], r_SA[pr, q, k, :], r_Arb[pr, 2 * k + q, tt, :])
                    close_bank("dve", last)
                    if c < NC - 1:
                        b = open_bank("dve")
                        for k in range(KD):
                            for q in range(2):
                                h, o2 = 2 * k + q, b[64 * q:64 * q + 64, k * HD:(k + 1) * HD]
                                mm(o2, r_bt[pr, tt, h * HD:(h + 1) * HD], r_SA[pr, q, k, :], True, False)
                                last = mm(o2, r_kt[pr, tt, h * HD:(h + 1) * HD], r_vt[pr, tt, h * HD:(h + 1) * HD], False, True)
                        close_bank("dve", last)
                note("gn")
                all_read_out()
                for j in range(4):
                    b = open_bank("dve")
                    close_bank("dve", mm(b[:, :], halves[:, :], arena[:, 12288 + NB * j:12288 + NB * (j + 1)]))
                for j in range(4):
                    pe.wait_ge(r_a2p, 4 + j + 1)
                    b = open_bank("act")
                    close_bank("act", mm(b[:, :], halves[:, :], arena[:, NB * j:NB * (j + 1)]))
                n = arrive(pe, ("g2",))
                for j in range(4):
                    b = open_bank("dve")
                    for u in range(2):
                        cc = slice((2 * j + u) * P, (2 * j + u + 1) * P)
                        mm(b[:, u * S:(u + 1) * S], slot(n)[:, 0:1024][:, cc], r_hgS[:, 0, :], True, False)
                        last = mm(b[:, u * S:(u + 1) * S], slot(n)[0:32, 1024:2048][:, cc], r_hgS[0:32, 1, :], False, True)
                    close_bank("dve", last)
                freed(("g2",), "dve")
                j0 = jobs["dve"]
                down(("rout",), KD, lambda k, tt: r_k[:, k, tt * P:(tt + 1) * P], lambda k: read_out("dve", j0 - 3 + k // 2), False)

            pe.wait_ge(ident_ready, 1)
            pe.wait_ge(vec_landed, 16 * n_vec_dmas)
            for v in range(NVT):
                r = min(P, NVEC - v * P)
                b = open_bank("act")
                close_bank("act", tr(b[:, 0:r], vrow[0:r, v, :], r))
            pe.wait_ge(consts, 1)
            modulation_a(0)
            for l in range(DEPTH):
                if l == 1:
                    modulation_b(l)
                norm(l, 0)
                if l > 1:
                    modulation_b(l)
                if l % 3 == 0:
                    mamba(l // 3)
                elif l % 3 == 1:
                    rwkv()
                else:
                    fox()
                if l == 0:
                    modulation_b(0)
                norm(l, 1)
                ffn(l)
                if l + 1 < DEPTH:
                    modulation_a(l + 1)

        @block.vector
        def _(dve):
            V = nc.vector
            counts = {}
            job = [0]

            def tell(ins, s=dve_step, hold=True):
                counts[s.name] = counts.get(s.name, 0) + 1
                ins.then_inc(s, 1)
                if hold:
                    dve.wait_ge(s, counts[s.name])

            def take():
                dve.wait_ge(dve_full, job[0] + 1)
                return psum_dve[job[0] % 2]

            def give(ins):
                job[0] += 1
                ins.then_inc(dve_free, 1)
                dve.wait_ge(dve_free, job[0])

            def flat(v):
                return v.rearrange("p a b -> p (a b)")

            def col(name, i, n=1):
                return vcol[:, COL[name] + i:COL[name] + i + n]

            def wide(name, i, n=KD):
                return col(name, i, n).unsqueeze(2).broadcast_to([P, n, S])

            def adaln(l, i):
                n = arrive(dve, ("ada", l, i))
                m, k4 = divmod(i, 4)
                if i == 0 or i == 8:
                    dve.wait_ge(ada_bias, 16 * (l + 1))
                for k in range(2):
                    for hf in range(2):
                        if (k, hf) == (0, 1) and counts.get("ada_slot_used"):
                            dve.wait_ge(ada_used, counts["ada_slot_used"])
                        o = ada[:, m * D + hf * NB:m * D + (hf + 1) * NB]
                        ins = V.scalar_tensor_tensor(out=o, in0=slot(n)[:, k * D + hf * NB:k * D + (hf + 1) * NB],
                                                     scalar=col("c", 2 * k4 + k), in1=o, op0=ALU.mult, op1=ALU.add)
                        if k == 1 and hf == 1:
                            tell(ins, ada_used, hold=False)
                        else:
                            counts["dve_step"] = counts.get("dve_step", 0) + 1
                            ins.then_inc(dve_step, 1)
                            dve.wait_ge(dve_step, counts["dve_step"] - (1 - k if hf == 0 else 1))
                release[n] = (ada_used, NADA * l + i + 1)

            at = {"load": 0, "unit": 0}
            keys = list(key_of)

            def stream(until):
                if not rwkv_done[0]:
                    until = min(until, before_rwkv)
                while at["load"] < len(loads):
                    n = at["load"]
                    if n in unit_of:
                        while at["unit"] < unit_of[n] + 2:
                            u = at["unit"]
                            if u >= until:
                                return
                            dve.wait_ge(hi_ready, u + 1)
                            raw = unit_view(n, u - unit_of[n])
                            o = w_lo[:, u % UNITS, :]
                            hi = w_hi[:, u % UNITS, :].bitcast(F32)
                            if len(raw.shape) == 3:
                                o, hi = (v.rearrange("p (k c) -> p k c", k=KD) for v in (o, hi))
                            tell(V.tensor_tensor(o, raw, hi, ALU.subtract), split_ready, hold=False)
                            at["unit"] += 1
                        release[n] = (split_ready, unit_of[n] + 2)
                    elif keys[n][0] == "ada":
                        if u_next(n) > until:
                            return
                        adaln(*keys[n][1:])
                    at["load"] += 1

            def u_next(n):
                while n < len(loads) and n not in unit_of:
                    n += 1
                return unit_of[n] if n in unit_of else n_units[0]
            rwkv_done = [False]

            def modulation_a(l):
                b = take()
                give(V.tensor_copy(mcol[:, 0:16], b[:, 0:16]))
                tell(V.scalar_tensor_tensor(out=nsc[:, 0, :], in0=mcol[:, 8:16], scalar=1.0,
                                            in1=col("norm1_w", l * KD, KD), op0=ALU.add, op1=ALU.mult), mod_ready)

            def modulation_b(l):
                for g in range(2):
                    for nh in range(2):
                        b = take()
                        give(V.tensor_scalar(gate[:, g, nh * NB:(nh + 1) * NB], b[:, :], 1.0, None, ALU.add))
                b = take()
                give(V.tensor_copy(mcol[:, 16:32], b[:, 0:16]))
                tell(V.scalar_tensor_tensor(out=nsc[:, 1, :], in0=mcol[:, 24:32], scalar=1.0,
                                            in1=col("norm2_w", l * KD, KD), op0=ALU.add, op1=ALU.mult), mod_ready)

            norms = [0]
            split_norms = [0]

            def norm(l, which):
                norms[0] += 1
                splits = (l, which) != (1, 0)
                for tt in range(TT):
                    dve.wait_ge(rstd_ready, 2 * norms[0] - 1 + tt)
                    tell(V.tensor_scalar(xn[:, tt, :], x[:, tt, :], small[:, 4 + tt:5 + tt], None, ALU.mult), xn_ready)
                for j in range(4):
                    if j % 2:
                        b = take()
                        for u in range(2):
                            k = 2 * j + u
                            ins = V.tensor_scalar(hT[:, k, :], b[:, u * S:(u + 1) * S], nsc[:, which, k:k + 1],
                                                  mcol[:, 16 * which + k:16 * which + k + 1], ALU.mult, ALU.add)
                            give(ins) if u else tell(ins)
                        if splits:
                            tell(V.tensor_copy(flat(h_hi2[which][:, 2 * j:2 * j + 2, :]), flat(hT[:, 2 * j:2 * j + 2, :])))
                    elif splits:
                        dve.wait_ge(h_hi_ready, 2 * split_norms[0] + j // 2 + 1)
                    if splits:
                        v = slice(2 * j, 2 * j + 2)
                        tell(V.tensor_tensor(flat(h_lo[:, v, :]), flat(hT[:, v, :]), flat(h_hi2[which][:, v, :]).bitcast(F32), ALU.subtract), h_split)
                if splits:
                    split_norms[0] += 1

            def split_narrow(i, width):
                dve.wait_ge(wdt_landed, 16 * i)
                tell(V.tensor_copy(wn_hi[:, :, 0:width], wnar[:, :, 0:width]))
                tell(V.tensor_tensor(wn_lo[:, :, 0:width], wnar[:, :, 0:width], wn_hi[:, :, 0:width].bitcast(F32), ALU.subtract), wn_split)

            res = [0]

            def residual(g):
                for tt in range(TT):
                    for nh in range(2):
                        b = psum_acc[2 * tt + nh]
                        dve.wait_ge(acc_full, 4 * res[0] + 2 * tt + nh + 1)
                        tell(V.tensor_tensor(b[:, :], b[:, :], gate[:, g, nh * NB:(nh + 1) * NB], ALU.mult))
                        xs = x[:, tt, nh * NB:(nh + 1) * NB]
                        tell(V.tensor_tensor(xs, xs, b[:, :], ALU.add), acc_free)
                res[0] += 1

            def ffn(l):
                f0 = first_unit("up", l, 0, 0)

                def low(i):
                    v = slice(2 * i, 2 * i + 2)
                    dve.wait_ge(g_hi_ready, KF // 2 * l + i + 1)
                    tell(V.tensor_tensor(flat(g_lo[:, v, :]), gx[:, i % 3, :], flat(g_hi[:, v, :]).bitcast(F32), ALU.subtract), g_split, hold=False)
                stream(f0 + UNITS)
                for i in range(KF // 2):
                    stream(f0 + 4 * i + 2 + UNITS)
                    b = take()
                    dve.wait_ge(act_free, mark[("ffn", l)][0] + i + 1)
                    give(V.tensor_tensor(gx[:, i % 3, :], gx[:, i % 3, :], b[:, :], ALU.mult))
                    if i:
                        low(i - 1)
                low(KF // 2 - 1)
                stream(first_unit("down2", l, 0) + KF + UNITS - 1)
                residual(1)

            def mamba(o):
                f0 = first_unit("xbc", o, 0)
                split_narrow(1 if o == 0 else 3, M_H)
                stream(f0 + UNITS)
                if o == 0:
                    dve.wait_ge(consts, 1)
                b = take()
                give(V.tensor_tensor(dtv[:, 0], b[:, 0:TT * M_H].rearrange("p (t h) -> p t h", t=TT),
                                     rowb[:, o * 32:o * 32 + 32].unsqueeze(1).broadcast_to([P, TT, M_H]), ALU.add))
                for j in range(16):
                    stream(f0 + 2 * j + UNITS)
                    b = take()
                    for tap in range(4):
                        sft = 3 - (3 - tap)
                        for u in range(2):
                            c = 2 * j + u
                            w = col("m_conv_w", o * 128 + (3 - tap) * 32 + c)
                            if tap == 0:
                                ins = V.tensor_scalar(xbcT[:, c, :], b[:, u * S:(u + 1) * S], w, col("m_conv_b", o * 32 + c),
                                                      ALU.mult, ALU.add)
                            else:
                                ins = V.scalar_tensor_tensor(out=xbcT[:, c, sft:S], in0=b[:, u * S:(u + 1) * S - sft], scalar=w,
                                                             in1=xbcT[:, c, sft:S], op0=ALU.mult, op1=ALU.add)
                            give(ins) if (tap == 3 and u == 1) else tell(ins)
                dve.wait_ge(dt_e, o + 1 if o == 0 else 3)
                tell(V.scalar_tensor_tensor(out=dtv[:, 3], in0=dtv[:, 0], scalar=0.0, in1=dtv[:, 2], op0=ALU.max, op1=ALU.add))
                tell(V.scalar_tensor_tensor(out=dtv[:, 4], in0=dtv[:, 3], scalar=-1.0,
                                            in1=rowb[:, 64 + o * 32:96 + o * 32].unsqueeze(1).broadcast_to([P, TT, M_H]),
                                            op0=ALU.mult, op1=ALU.mult), a_ready)
                for j in range(8):
                    b = take()
                    for tt in range(TT):
                        ins = V.tensor_tensor(xd[:, tt, 256 * j:256 * j + 256].rearrange("p (h d) -> p h d", h=4),
                                              b[:, tt * 256:(tt + 1) * 256].rearrange("p (h d) -> p h d", h=4),
                                              dtv[:, 3, tt, 4 * j:4 * j + 4].unsqueeze(2).broadcast_to([P, 4, HD]), ALU.mult)
                        give(ins) if tt else tell(ins)
                for g in range(M_G):
                    b = take()
                    give(V.tensor_tensor(scT[:, g, :], b[:, 0:384], upto[:, :], ALU.mult))
                a0 = mark[("head", o)][0]

                def pair_out(p):
                    b = take()
                    give(V.scalar_tensor_tensor(out=xbcT[:, p, :], in0=xbcT[:, p, :], scalar=dskip[:, o, p:p + 1],
                                                in1=b[:, 0:256], op0=ALU.mult, op1=ALU.add))
                for h in range(M_H):
                    if h >= 4 and h % 2 == 0:
                        pair_out((h - 4) // 2)
                    dve.wait_ge(act_free, a0 + h + 1)
                    tell(V.tensor_tensor(gm[:, h % 4, :], dec[:, h % 3, :], scT[:, h // 4, :], ALU.mult), gmat_ready)
                pair_out(14)
                pair_out(15)
                for g in range(M_G):
                    stream(f0 + 32 + 2 * g + UNITS)
                    dve.wait_ge(act_free, mark[("z", o)][0] + g + 1)
                    tell(V.tensor_tensor(flat(xbcT[:, 2 * g:2 * g + 2, :]), flat(xbcT[:, 2 * g:2 * g + 2, :]), zs[:, g % 2, :], ALU.mult), yz_ready)
                for g in range(M_G):
                    dve.wait_ge(rs_ready, M_G * o + g + 1)
                    for u in range(2):
                        c = 2 * g + u
                        tell(V.scalar_tensor_tensor(out=xbcT[:, c, :], in0=xbcT[:, c, :], scalar=col("m_norm_w", o * 16 + c),
                                                    in1=rsm[:, g % 2, :], op0=ALU.mult, op1=ALU.mult), yn_done if u else dve_step)
                    v = slice(2 * g, 2 * g + 2)
                    tell(V.tensor_copy(flat(y_hi[:, v, :]), flat(xbcT[:, v, :])))
                    tell(V.tensor_tensor(flat(y_lo[:, v, :]), flat(xbcT[:, v, :]), flat(y_hi[:, v, :]).bitcast(F32), ALU.subtract), yn_ready)
                stream(first_unit("mout", o, 0) + M_KT + UNITS - 1)

            def fox():
                f0 = first_unit("qkv", 0)
                split_narrow(2, R_H)
                stream(f0 + UNITS)
                b = take()
                give(V.tensor_tensor(ffv[:, 0], b[:, 0:TT * R_H].rearrange("p (t h) -> p t h", t=TT),
                                     rowb[:, 128:144].unsqueeze(1).broadcast_to([P, TT, R_H]), ALU.add))
                dve.wait_ge(dt_e, 2)
                tell(V.scalar_tensor_tensor(out=ffv[:, 3], in0=ffv[:, 0], scalar=0.0, in1=ffv[:, 2], op0=ALU.min, op1=ALU.subtract), a_ready)
                for i in range(8):
                    stream(f0 + 2 * i + 2 + UNITS)
                    dve.wait_ge(f_rs, i + 1)
                    m, j = i // 4, i % 4
                    v = flat(fqk[:, m, 2 * j:2 * j + 2, :])
                    tell(V.scalar_tensor_tensor(out=v, in0=v, scalar=qkw[:, m:m + 1], in1=frs[:, i % 2, :], op0=ALU.mult, op1=ALU.mult), f_qk)
                for i in range(4):
                    stream(f0 + 16 + 2 * i + UNITS)
                    b = take()
                    give(V.tensor_copy(fv[:, :, 256 * i:256 * i + 256], b[:, :].rearrange("p (t d) -> p t d", t=TT)))
                a0 = mark["foxhead"][0]

                def normalise(h):
                    dve.wait_ge(f_exp, h + 1)
                    tell(V.reciprocal(fst[:, 3, :, h], fst[:, 2, :, h]))
                    for blk, r in enumerate((slice(0, P), slice(P, 384))):
                        tell(V.tensor_scalar(flg[:, h % 4, r], flg[:, h % 4, r], fst[:, 3, blk, h:h + 1], None, ALU.mult), f_norm if blk else dve_step)
                for h in range(R_H + 4):
                    if h < R_H:
                        b = take()
                        if h >= 4:
                            dve.wait_ge(act_full, a0 + h - 3)
                        for blk, r in enumerate((slice(0, P), slice(P, 384))):
                            ins = V.tensor_tensor_reduce(flg[:, h % 4, r], b[:, r], neg[:, r], 1.0, -3e38, ALU.add, ALU.max,
                                                         fst[:, 0, blk, h:h + 1])
                            give(ins) if blk else tell(ins)
                        tell(V.tensor_scalar(fst[:, 1, :, h], fst[:, 0, :, h], -1.0, None, ALU.mult), f_max)
                    if 1 <= h < R_H + 1:
                        normalise(h - 1)
                    if h >= 4 and h % 2 == 0:
                        b = take()
                        p = (h - 4) // 2
                        tell(V.tensor_copy(o_hi[:, p, :], b[:, 0:256]))
                        give(V.tensor_tensor(o_lo[:, p, :], b[:, 0:256], o_hi[:, p, :].bitcast(F32), ALU.subtract))
                stream(first_unit("fout", 0) + KD + UNITS - 1)

            def rwkv():
                m0 = mark["rwkv"][0]
                rs = r_hid[:, 2, :]
                dve.wait_ge(act_free, mark[("norm", 1, 0)][0] + 2)
                tell(V.memset(rs, 1.0))
                tell(V.memset(rs.rearrange("p (c t) -> p c t", t=CH)[:, :, 0:1], 0.0))
                tell(V.tensor_tensor(r_dx[:, :, 1:S], hT[:, :, 0:S - 1], hT[:, :, 1:S], ALU.subtract))
                tell(V.tensor_scalar(r_dx[:, :, 0:1], hT[:, :, 0:1], -1.0, None, ALU.mult))
                waits = [0, 0, m0 + 1, m0 + 2, 0, 0]
                for n, (mi, buf) in enumerate(zip((3, 4, 5, 1, 0, 2), (r_xsA, r_xsB, r_xsA, r_xsB, r_xsR, r_xsV))):
                    if waits[n]:
                        dve.wait_ge(act_full, waits[n])
                    for k in range(KD):
                        tell(V.scalar_tensor_tensor(out=buf[:, k, :], in0=r_dx[:, k, :], scalar=col("r_mix", mi * KD + k),
                                                    in1=hT[:, k, :], op0=ALU.mult, op1=ALU.add), xs_ready if k == KD - 1 else dve_step)
                dve.wait_ge(act_free, m0 + 11)
                for k in range(KD):
                    tell(V.tensor_tensor_scan(r_dx[:, k, :], rs, r_s[:, k, :], 0.0, ALU.mult, ALU.add))
                tell(V.tensor_tensor(r_s[:, :, :], r_dx[:, :, :], r_s[:, :, :], ALU.subtract), r_v2a)
                for j in range(4):
                    b = take()
                    v = slice(2 * j, 2 * j + 2)
                    give(V.tensor_copy(flat(r_k[:, v, :]), b[:, :]))
                    tell(V.tensor_tensor(r_xsA[:, v, :], r_k[:, v, :], wide("r_k_k", 2 * j, 2), ALU.mult), r_v2a)
                dve.wait_ge(r_a2v, 5)
                tell(V.tensor_scalar(flat(r_xsB), flat(r_xsB), 1e-12, None, ALU.max))
                tell(V.reciprocal(flat(r_xsB), flat(r_xsB)))
                tell(V.tensor_tensor(flat(r_xsA), flat(r_xsA), flat(r_xsB), ALU.mult))
                tell(V.scalar_tensor_tensor(out=r_xsB[:, :, :], in0=r_a[:, :, :], scalar=-1.0, in1=wide("r_k_a", 0), op0=ALU.add, op1=ALU.mult))
                tell(V.scalar_tensor_tensor(out=flat(r_k), in0=flat(r_xsB), scalar=1.0, in1=flat(r_k), op0=ALU.add, op1=ALU.mult), r_v2a)
                tell(V.scalar_tensor_tensor(out=flat(r_s), in0=flat(r_xsA), scalar=-1.0, in1=flat(r_s), op0=ALU.mult, op1=ALU.mult))
                tell(V.tensor_tensor(flat(r_xsA), flat(r_xsA), flat(r_a), ALU.mult))
                dve.wait_ge(r_a2v, 6)
                tell(V.tensor_tensor(flat(r_xsA), flat(r_xsA), flat(r_xsB), ALU.mult))
                tell(V.tensor_tensor(flat(r_a), flat(r_r), flat(r_k), ALU.mult))
                tell(V.tensor_tensor(r_a[:, :, :], r_a[:, :, :], wide("r_r_k", 0), ALU.mult), r_v2p)
                tell(V.tensor_tensor(flat(r_k), flat(r_k), flat(r_xsB), ALU.mult))
                dve.wait_ge(r_a2v, 7)
                tell(V.tensor_copy(pend[:, :, :], r_dx[:, :, CH - 1:S:CH]))
                tell(V.tensor_tensor(flat(r_r), flat(r_r), flat(r_dx), ALU.mult), r_v2p)
                for j in range(4):
                    b = take()
                    v = flat(r_v[:, 2 * j:2 * j + 2, :])
                    give(V.tensor_tensor(v, v, b[:, :], ALU.mult))

                def blocks(b):
                    return b[:, :].rearrange("p (c d) -> p c d", c=4)

                def own(v, B, q, pr):
                    return v[pr, 4 * B + q:4 * B + q + 3:2, :, :]

                def diag(src, par):
                    pr = slice(64 * par, 64 * par + 64)
                    return src[pr].rearrange("p (i t) d -> p i t d", i=2)[:, :, :, 64 * par:64 * par + 64]

                def ns(B, q, lv, s=ns_ready):
                    tell(V.tensor_tensor(wk[q][1][:, :, :], wk[q][0][:, :, :], level[:, lv, :].unsqueeze(1).broadcast_to([P, 4, P]), ALU.mult), ns_ready)
                eye = ident[:, :].unsqueeze(1).broadcast_to([P, 4, P])
                for B in range(4):
                    for q in range(2):
                        b = take()
                        give(V.tensor_copy(flat(wk[q][0]), b[:, :]))
                        b = take()
                        for par in range(2):
                            pr = slice(64 * par, 64 * par + 64)
                            ms = upto_c[pr, 64 * par:64 * par + 64].unsqueeze(1).unsqueeze(1).broadcast_to([64, 2, 2, 64])
                            ins = V.tensor_tensor(own(r_Arb, B, q, pr), diag(blocks(b), par), ms, ALU.mult)
                            give(ins) if par else tell(ins)
                        for m, ms in enumerate((before_c, upto_c)):
                            b = take()
                            give(V.tensor_tensor(r_mk[q][m][:, :, :], blocks(b), ms[:, :].unsqueeze(1).broadcast_to([P, 4, P]), ALU.mult))
                    for q in range(2):
                        ns(B, q, 0)
                    for q in range(2):
                        tell(V.tensor_tensor(wk[q][2][:, :, :], wk[q][1][:, :, :], eye, ALU.add))
                    for q in range(2):
                        b = take()
                        give(V.tensor_tensor(wk[q][3][:, :, :], blocks(b), eye, ALU.add))
                        ns(B, q, 1)
                    for lv in range(1, 6):
                        for q in range(2):
                            b = take()
                            if lv < 5:
                                for m in (3, 2):
                                    if m == 2:
                                        b = take()
                                    give(V.tensor_tensor(flat(wk[q][m]), flat(wk[q][m]), b[:, :], ALU.add))
                                ns(B, q, lv + 1)
                            else:
                                if B == 3 and q == 1:
                                    tell(V.memset(r_S[:, :, :], 0.0))
                                for par in range(2):
                                    pr = slice(64 * par, 64 * par + 64)
                                    ins = V.tensor_tensor(own(r_XT4, B, q, pr), diag(wk[q][3], par), diag(blocks(b), par), ALU.add)
                                    give(ins) if par else tell(ins)
                dve.wait_ge(act_free, mark["chunks"][0])
                for c in range(NC):
                    tt, par = c // 2, c % 2
                    pr = slice(64 * par, 64 * par + 64)
                    cs = slice(c * CH, (c + 1) * CH)

                    def heads8(b, r):
                        return b[r, :].rearrange("p (k d) -> p k d", k=KD)
                    for q in range(2):
                        b = take()
                        give(V.tensor_tensor(r_R[pr, q, :, :], heads8(b, pr), r_U[pr, :, tt, 64 * q:64 * q + 64], ALU.add))
                    for q in range(2):
                        b = take()
                        qr = slice(64 * q, 64 * q + 64)
                        give(V.tensor_tensor(r_k[qr, :, cs], r_k[qr, :, cs], heads8(b, qr), ALU.add))
                    b = take()
                    give(V.tensor_tensor(r_k[:, :, cs], r_k[:, :, cs], heads8(b, slice(0, P)), ALU.add))
                    if c < NC - 1:
                        b = take()
                        tell(V.tensor_tensor(flat(r_S), flat(r_S), b[:, :], ALU.add))
                        give(V.tensor_tensor(r_S[:, :, :], r_S[:, :, :], pend[:, :, c:c + 1].broadcast_to([P, KD, HD]), ALU.mult))
                for j in range(4):
                    b = take()
                    v = flat(r_k[:, 2 * j:2 * j + 2, :])
                    give(V.scalar_tensor_tensor(out=v, in0=b[:, :], scalar=-1.0 / HD, in1=v, op0=ALU.mult, op1=ALU.add))
                for j in range(4):
                    dve.wait_ge(r_a2v, 8 + j)
                    v = flat(r_k[:, 2 * j:2 * j + 2, :])
                    tell(V.tensor_tensor(v, v, flat(r_dx[:, 2 * j:2 * j + 2, :]), ALU.mult))
                    for u in range(2):
                        k = 2 * j + u
                        tell(V.tensor_scalar(r_k[:, k, :], r_k[:, k, :], col("r_lnx_w", k), col("r_lnx_b", k), ALU.mult, ALU.add))
                    tell(V.tensor_tensor(v, v, flat(r_v[:, 2 * j:2 * j + 2, :]), ALU.add))
                    b = take()
                    give(V.tensor_tensor(v, v, b[:, :], ALU.mult))

            dve.wait_ge(row_landed, 16 * N_ROWS)
            tell(V.tensor_scalar(qkw[:, 0:1], qkw[:, 0:1], HD ** -0.5, None, ALU.mult))
            dve.wait_ge(cond_ready, 1)
            stream(0)
            modulation_a(0)
            for l in range(DEPTH):
                if l == 1:
                    modulation_b(l)
                norm(l, 0)
                if l > 1:
                    modulation_b(l)
                if l % 3 == 0:
                    mamba(l // 3)
                elif l % 3 == 1:
                    rwkv()
                    rwkv_done[0] = True
                else:
                    fox()
                if l == 0:
                    modulation_b(0)
                residual(0)
                norm(l, 1)
                ffn(l)
                if l + 1 < DEPTH:
                    modulation_a(l + 1)

        @block.scalar
        def _(act):
            A = nc.scalar.activation
            counts = {}
            job = [0]

            def tell(ins, s=act_step):
                counts[s.name] = counts.get(s.name, 0) + 1
                ins.then_inc(s, 1)
                act.wait_ge(s, counts[s.name])

            def take():
                act.wait_ge(act_full, job[0] + 1)
                return psum_act[job[0] % 2]

            def give(ins):
                job[0] += 1
                ins.then_inc(act_free, 1)
                act.wait_ge(act_free, job[0])

            def flat(v):
                return v.rearrange("p a b -> p (a b)")

            def col(name, i):
                return vcol[:, COL[name] + i:COL[name] + i + 1]
            at = [0, 0]
            split_loads = sorted(unit_of)
            rwkv_done = [False]

            def stream(until):
                if not rwkv_done[0]:
                    until = min(until, before_rwkv)
                while at[0] < min(until, n_units[0]):
                    u = at[0]
                    n = split_loads[u // 2]
                    if u % 2 == 0:
                        act.wait_ge(landed[n % RING], arrive_at[n])
                    if u >= UNITS:
                        act.wait_ge(*unit_release[u - UNITS])
                    o = w_hi[:, u % UNITS, :]
                    raw = unit_view(n, u % 2)
                    if len(raw.shape) == 3:
                        o = o.rearrange("p (k c) -> p k c", k=KD)
                    tell(A(o, raw, ACT.Copy), hi_ready)
                    at[0] += 1
            norms = [0]

            def norm(l, which):
                if norms[0] == 0:
                    act.wait_ge(x_landed, 16)
                for tt in range(TT):
                    for nh in range(2):
                        if norms[0]:
                            act.wait_ge(acc_free, 4 * norms[0] - 3 + 2 * tt + nh)
                        r = slice(nh * NB, (nh + 1) * NB)
                        tell(A(xn[:, tt, r], x[:, tt, r], ACT.Square, accum_out=small[:, nh:nh + 1]))
                    tell(A(small[:, 2:3], small[:, 0:1], ACT.Identity, bias=small[:, 1:2]))
                    tell(A(small[:, 3:4], small[:, 2:3], ACT.Ln, scale=1.0 / D, bias=epsc[:, 0:1]))
                    tell(A(small[:, 4 + tt:5 + tt], small[:, 3:4], ACT.Exp, scale=-0.5), rstd_ready)
                act.wait_ge(mod_ready, 2 * l + 1 + which)
                for j in (0, 2):
                    b = take()
                    for u in range(2):
                        k = 2 * j + u
                        ins = A(hT[:, k, :], b[:, u * S:(u + 1) * S], ACT.Identity, scale=nsc[:, which, k:k + 1],
                                bias=mcol[:, 16 * which + k:16 * which + k + 1])
                        give(ins) if u else tell(ins)
                    if (l, which) != (1, 0):
                        tell(A(flat(h_hi2[which][:, 2 * j:2 * j + 2, :]), flat(hT[:, 2 * j:2 * j + 2, :]), ACT.Copy), h_hi_ready)
                norms[0] += 1

            def ffn(l):
                f0 = first_unit("up", l, 0, 0)

                def high(i):
                    act.wait_ge(dve_free, mark[("ffn", l)][1] + i + 1)
                    tell(A(flat(g_hi[:, 2 * i:2 * i + 2, :]), gx[:, i % 3, :], ACT.Copy), g_hi_ready)
                for i in range(KF // 2):
                    stream(f0 + 4 * i + UNITS)
                    b = take()
                    if i >= 3:
                        act.wait_ge(g_split, KF // 2 * l + i - 2)
                    give(A(gx[:, i % 3, :], b[:, :], ACT.Silu))
                    stream(f0 + 4 * i + 2 + UNITS)
                    if i:
                        high(i - 1)
                high(KF // 2 - 1)
                stream(first_unit("down2", l, 0) + KF + UNITS - 1)

            def log1p_exp(v):
                tell(A(v[:, 1], v[:, 0], ACT.Abs))
                tell(A(v[:, 2], v[:, 1], ACT.Exp, scale=-1.0))
                tell(A(v[:, 2], v[:, 2], ACT.Ln, bias=epsc[:, 2:3]), dt_e)

            def mamba(o):
                f0 = first_unit("xbc", o, 0)
                stream(f0 + UNITS)
                act.wait_ge(dve_free, mark[("mamba", o)][1] + 1)
                log1p_exp(dtv)
                for j in range(16):
                    stream(f0 + 2 * j + 2 + UNITS)
                    act.wait_ge(dve_free, mark[("conv", o)][1] + j + 1)
                    v = flat(xbcT[:, 2 * j:2 * j + 2, :])
                    tell(A(v, v, ACT.Silu), xbc_silu)

                def seg(h):
                    for tt in range(TT):
                        tell(A(segw[:, h % 2, tt, :], after[:, :], ACT.Copy, scale=dtv[:, 4, tt, h:h + 1]), seg_ready if tt else act_step)
                act.wait_ge(a_ready, 1 if o == 0 else 3)
                seg(0)
                seg(1)
                for h in range(M_H):
                    b = take()
                    if h >= 3:
                        act.wait_ge(gmat_ready, M_H * o + h - 2)
                    give(A(dec[:, h % 3, :], b[:, 0:384], ACT.Exp))
                    if h + 2 < M_H:
                        seg(h + 2)
                for g in range(M_G + 1):
                    if g < M_G:
                        stream(f0 + 32 + 2 * g + UNITS)
                        b = take()
                        if g == 0:
                            act.wait_ge(gmat_ready, M_H * (o + 1))
                        if g >= 2:
                            act.wait_ge(yz_ready, M_G * o + g - 1)
                        give(A(zs[:, g % 2, :], b[:, :], ACT.Silu))
                    if g:
                        act.wait_ge(yz_ready, M_G * o + g)
                        tell(A(flat(sqz[:, 2 * g - 2:2 * g, :]), flat(xbcT[:, 2 * g - 2:2 * g, :]), ACT.Square), sq_ready)
                for g in range(M_G):
                    b = take()
                    if g >= 2:
                        act.wait_ge(yn_done, M_G * o + g - 1)
                    give(A(rsm[:, g % 2, :], b[:, 0:256], ACT.Ln, scale=1.0 / 256, bias=epsc[:, 0:1]))
                    tell(A(rsm[:, g % 2, :], rsm[:, g % 2, :], ACT.Exp, scale=-0.5), rs_ready)
                stream(first_unit("mout", o, 0) + M_KT + UNITS - 1)

            def fox():
                f0 = first_unit("qkv", 0)
                stream(f0 + UNITS)
                act.wait_ge(dve_free, mark["fox"][1] + 1)
                log1p_exp(ffv)

                def project(i):
                    b = take()
                    m, j = i // 4, i % 4
                    tell(A(fsq[:, i % 2, :], b[:, :], ACT.Square), f_sq)
                    give(A(flat(fqk[:, m, 2 * j:2 * j + 2, :]), b[:, :], ACT.Copy))

                def inv_rms(i):
                    b = take()
                    if i >= 2:
                        act.wait_ge(f_qk, i - 1)
                    give(A(frs[:, i % 2, :], b[:, :], ACT.Ln, scale=1.0 / HD, bias=epsc[:, 0:1]))
                    tell(A(frs[:, i % 2, :], frs[:, i % 2, :], ACT.Exp, scale=-0.5), f_rs)
                for i in range(8):
                    stream(f0 + 2 * i + UNITS)
                    project(i)
                    stream(f0 + 2 * i + 2 + UNITS)
                    if i:
                        inv_rms(i - 1)
                inv_rms(7)
                stream(f0 + 24 + UNITS - 1)
                d0 = mark["foxhead"][1]

                def seg(h):
                    tell(A(fsegw[:, h % 2, 0:P], after[:, :], ACT.Copy, scale=ffv[:, 3, 0, h:h + 1]))
                    tell(A(fsegw[:, h % 2, P:2 * P], ones[:, :], ACT.Copy, scale=ffv[:, 3, 1, h:h + 1]))
                    tell(A(fsegw[:, h % 2, 2 * P:], after[:, :], ACT.Copy, scale=ffv[:, 3, 1, h:h + 1]), seg_ready)
                act.wait_ge(a_ready, 2)
                seg(0)
                seg(1)
                for h in range(R_H + 2):
                    if h < R_H:
                        act.wait_ge(f_max, h + 1)
                        if h + 2 < R_H:
                            seg(h + 2)
                        for blk, r in enumerate((slice(0, P), slice(P, 384))):
                            tell(A(flg[:, h % 4, r], flg[:, h % 4, r], ACT.Exp, bias=fst[:, 1, blk, h:h + 1],
                                   accum_out=fst[:, 2, blk, h:h + 1]), f_exp if blk else act_step)
                    if h >= 2:
                        hh = h - 2
                        b = take()
                        if hh >= 4:
                            p = (hh - 4) // 2
                            act.wait_ge(dve_full, d0 + min(2 * p + 5, R_H) + p + 1)
                        give(A(fpT[:, hh % 4, :], b[:, 0:384], ACT.Copy))
                stream(first_unit("fout", 0) + KD + UNITS - 1)

            def rwkv():
                b = take()
                give(A(r_hid[0:64, 0, :], b[0:64, 0:S], ACT.Tanh))
                b = take()
                give(A(r_hid[64:128, 0, :], b[64:128, 0:S], ACT.Copy))
                b = take()
                tell(A(r_hgS[:, 0, :], b[:, 0:S], ACT.Sigmoid))
                give(A(r_hgS[0:32, 1, :], b[0:32, S:2 * S], ACT.Sigmoid))
                for m, (dst, w) in enumerate(((r_s, "r_w0"), (r_a, "r_a0"))):
                    for j in range(4):
                        b = take()
                        for u in range(2):
                            k = 2 * j + u
                            ins = A(dst[:, k, :], b[:, u * S:(u + 1) * S], ACT.Sigmoid, bias=col(w, k))
                            give(ins) if u else tell(ins)
                def features(dst, j):
                    b = take()
                    give(A(flat(dst[:, 2 * j:2 * j + 2, :]), b[:, :], ACT.Copy))

                def tokens(dst):
                    for j in range(4):
                        b = take()
                        give(A(dst[:, :, 256 * j:256 * j + 256], b[:, :].rearrange("p (t d) -> p t d", t=TT), ACT.Copy))
                act.wait_ge(r_v2a, 1)
                tell(A(flat(r_s), flat(r_s), ACT.Exp, scale=-E_HALF), r_a2v)
                for j in range(4):
                    act.wait_ge(r_v2a, 2 + j)
                    if j == 0:
                        act.wait_ge(dve_free, mark["kproj"][1] + 4)
                    tell(A(flat(r_xsB[:, 2 * j:2 * j + 2, :]), flat(r_xsA[:, 2 * j:2 * j + 2, :]), ACT.Square), r_a2p)
                features(r_r, 0)
                features(r_r, 1)
                for j in range(4):
                    b = take()
                    give(A(flat(r_xsB[:, 2 * j:2 * j + 2, :]), b[:, :], ACT.Sqrt))
                    tell(A(small[:, 6:7], epsc[:, 2:3], ACT.Copy), r_a2v)
                features(r_r, 2)
                features(r_r, 3)
                act.wait_ge(r_v2a, 6)
                tell(A(flat(r_xsB), flat(r_dx), ACT.Exp, scale=E_HALF), r_a2v)
                tell(A(flat(r_dx), flat(r_dx), ACT.Exp, scale=-E_HALF), r_a2v)
                for j in range(4):
                    features(r_v, j)
                tokens(r_vt)
                tokens(r_bt)
                tokens(r_kt)
                for B in range(4):
                    for q in range(2):
                        b = take()
                        give(A(r_U[:, 2 * B:2 * B + 2, :, 64 * q:64 * q + 64],
                               b[:, 0:256].rearrange("p (i t d) -> p i t d", i=2, t=2), ACT.Copy))
                        b = take()
                        qr = slice(64 * q, 64 * q + 64)
                        give(A(flat(r_k[qr, 2 * B:2 * B + 2, :]), b[qr, :], ACT.Copy))
                    for lv in range(1, 6):
                        for q in range(2):
                            b = take()
                            give(A(flat(wk[q][4]), b[:, :], ACT.Copy))
                for c in range(NC):
                    pr = slice(64 * (c % 2), 64 * (c % 2) + 64)
                    for q in range(2):
                        b = take()
                        give(A(flat(r_SA[pr, q, :, :]), b[pr, :], ACT.Copy))
                for j in range(4):
                    act.wait_ge(dve_free, mark["gn"][1] + j + 1)
                    tell(A(flat(r_dx[:, 2 * j:2 * j + 2, :]), flat(r_k[:, 2 * j:2 * j + 2, :]), ACT.Square), r_a2p)
                for j in range(4):
                    b = take()
                    v = flat(r_dx[:, 2 * j:2 * j + 2, :])
                    give(A(v, b[:, :], ACT.Ln, scale=1.0 / HD, bias=epsc[:, 1:2]))
                    tell(A(v, v, ACT.Exp, scale=-0.5), r_a2v)

            for name, r, m, p0, tile in vector_parts():
                src = t[name].rearrange(VEC_LAYOUT[name]).rearrange("(r p) -> r p", p=P)
                act.dma_start(vrow[p0:p0 + m, tile, :], src[r:r + m, :]).then_inc(vec_landed, 16)
            for i, (dst, src) in enumerate((
                    (rowb[:, 0:64], t["m_dt_bias"].rearrange("a h -> (a h)").partition_broadcast(P)),
                    (rowb[:, 64:128], t["m_A_log"].rearrange("a h -> (a h)").partition_broadcast(P)),
                    (rowb[:, 128:144], t["f_fgate_b"].rearrange("a h -> (a h)").partition_broadcast(P)),
                    (qkw[0:64, 0:1], t["f_q_norm_w"].rearrange("a h -> h a")), (qkw[64:128, 0:1], t["f_q_norm_w"].rearrange("a h -> h a")),
                    (qkw[0:64, 1:2], t["f_k_norm_w"].rearrange("a h -> h a")), (qkw[64:128, 1:2], t["f_k_norm_w"].rearrange("a h -> h a")),
                    (dskip[0:64, :, :].rearrange("p a b -> p (a b)"), t["m_D"].rearrange("a (c two) -> two (a c)", two=2)[0].partition_broadcast(64)),
                    (dskip[64:128, :, :].rearrange("p a b -> p (a b)"), t["m_D"].rearrange("a (c two) -> two (a c)", two=2)[1].partition_broadcast(64)))):
                with nc.allow_non_contiguous_dma(reason="a few columns"):
                    act.dma_start(dst, src).then_inc(row_landed, 16)
            for v in range(NVT):
                b = take()
                r = min(P, NVEC - v * P)
                give(A(vcol[:, v * P:v * P + r], b[:, 0:r], ACT.Copy))
            tell(A(vcol[:, 0:KD], vcol[:, 0:KD], ACT.Silu), cond_ready)
            act.wait_ge(row_landed, 16 * N_ROWS)
            tell(A(rowb[:, 64:128], rowb[:, 64:128], ACT.Exp))
            act.wait_ge(consts, 1)
            for l in range(DEPTH):
                norm(l, 0)
                if l % 3 == 0:
                    mamba(l // 3)
                elif l % 3 == 1:
                    rwkv()
                    rwkv_done[0] = True
                else:
                    fox()
                norm(l, 1)
                ffn(l)

        @block.gpsimd
        def _(pool):
            G = nc.gpsimd
            n = [0]

            def done(ins):
                n[0] += 1
                ins.then_inc(pool_step, 1)
                pool.wait_ge(pool_step, n[0])

            def select(v, pattern, base, mult, fill=0.0, op=ALU.is_ge):
                done(G.affine_select(out=v, in_=v, compare_op=op, fill=fill, base=base, pattern=pattern, channel_multiplier=mult))

            done(G.memset(ident[:, :], 0.0))
            G.affine_select(out=ident[:, :], in_=ident[:, :], compare_op=ALU.not_equal, fill=1.0, base=0,
                            pattern=[[-1, P]], channel_multiplier=1).then_inc(ident_ready, 1)
            done(G.memset(ada[:, :], 0.0))
            pool.dma_start(ada[0:1, :], t["ada_b"][0:1, :]).then_inc(ada_bias, 16)
            pool.dma_start(wnar[:, :, :], t["m_in_w"][0][:, M_IN + M_XBC:].rearrange("(k p) n -> p k n", p=P)).then_inc(wdt_landed, 16)
            done(G.memset(ones[:, :], 1.0))
            done(G.memset(halves[:, :], 0.0))
            done(G.memset(halves[0:64, 0:64], 1.0))
            done(G.memset(halves[64:128, 64:128], 1.0))
            done(G.memset(upto[:, :], 1.0))
            select(upto[:, 0:256], [[1, 256]], 0, -1)
            select(upto[:, 256:384], [[1, P]], 0, -1)
            done(G.memset(after[:, :], 1.0))
            select(after[:, :], [[-1, P]], -1, 1)
            done(G.memset(neg[:, :], 0.0))
            select(neg[:, 0:P], [[-1, P]], 0, 1, NEG)
            select(neg[:, 256:384], [[-1, P]], 0, 1, NEG)
            done(G.memset(epsc[:, 0:1], EPS))
            done(G.memset(epsc[:, 1:2], R_GN_EPS))
            done(G.memset(epsc[:, 2:3], 1.0))
            for m, dlt in ((before_c, -1), (upto_c, 0)):
                done(G.tensor_copy(m[:, :], halves[:, :]))
                select(m[:, :], [[1, P]], dlt, -1)
            for lv in range(6):
                s = 1 << lv
                done(G.memset(level[:, lv, :], 0.0))
                v = level[:, lv, :].rearrange("p (b r) -> p b r", r=2 * s)[:, :, 0:s]
                done(G.memset(v, 1.0))
                select(v, [[-2 * s, P // (2 * s)], [0, s]], -s, 1)
                select(v, [[2 * s, P // (2 * s)], [0, s]], 2 * s - 1, -1)
            G.memset(small[:, 6:8], 0.0).then_inc(consts, 1)
            for l in range(1, DEPTH):
                pool.wait_ge(acc_free, 8 * l - 4)
                if l == 1:
                    pool.dma_start(wnar[:, :, 0:R_H], t["f_qkvf_w"][0][:, 3 * D:].rearrange("(k p) n -> p k n", p=P)).then_inc(wdt_landed, 16)
                if l == 3:
                    pool.dma_start(wnar[:, :, :], t["m_in_w"][1][:, M_IN + M_XBC:].rearrange("(k p) n -> p k n", p=P)).then_inc(wdt_landed, 16)
                done(G.memset(ada[:, :], 0.0))
                pool.dma_start(ada[0:1, :], t["ada_b"][l:l + 1, :]).then_inc(ada_bias, 16)

        @block.sync
        def _(sp):
            sp.dma_start(x[:, :, :], t["x"][0].rearrange("(t p) d -> p t d", p=P)).then_inc(x_landed, 16)
            for n, parts in enumerate(loads):
                if n >= RING:
                    sp.wait_ge(*release[n - RING])
                for cols, src, who, w in parts:
                    if isinstance(who, tuple):
                        dst = slot(n)[who[0]:who[1], cols]
                    else:
                        dst = slot(n)[:, cols].rearrange("p (k c) -> p k c", c=w)
                    sp.dma_start(dst, src).then_inc(landed[n % RING], 16)
            sp.wait_ge(acc_free, 8 * DEPTH)
            sp.dma_start(out[0].rearrange("(t p) d -> p t d", p=P), x[:, :, :]).then_inc(out_landed, 16)
            sp.wait_ge(out_landed, 16)


_OUTS = [((1, S, D), 'float32')]


def kernel(**inputs):
    import numpy as _np
    import concourse.bacc as _bacc
    from concourse import mybir as _mybir
    from concourse.bass_utils import run_bass_kernel_spmd as _run

    nc = _bacc.Bacc("TRN2", target_bir_lowering=False, num_devices=1)
    arrays, args = {}, {}
    for name in inputs:
        a = _np.ascontiguousarray(inputs[name])
        arrays[f"in_{name}_dram"] = a
        args[name] = nc.dram_tensor(f"in_{name}_dram", a.shape, _mybir.dt.from_np(a.dtype), kind="ExternalInput").ap()
    outs = []
    for i, (shape, dtype) in enumerate(_OUTS):
        dt = _mybir.dt.from_np(_np.dtype(dtype))
        outs.append(nc.dram_tensor(f"out_{i}_dram", shape, dt, kind="ExternalOutput").ap())
    trunk(nc, args, outs[0])
    r = _run(nc, [arrays], core_ids=[0])
    return r.results[0]["out_0_dram"]
```
